# Optimizing a Trainium2 kernel written in Bass

```python
import math
import jax, jax.numpy as jnp
from jax import lax
import numpy as np

D_MODEL = 1024
BATCH = 1
SEQ = 512
DEPTH = 2

HEAD_DIM = 64
GRID_W = 64
ROPE_THETA = 10000.0
EPS = 1e-6
BLOCK = 128
NEG = -1e30

WIN_HEADS = 4
WIN_KV = 2
WIN_RADIUS = 128
AX_HEADS = 4
AX_KV = 2
DIL_HEADS = 4
DIL_KV = 2
DIL_PATTERNS = ((128, 1), (512, 4), (2048, 16))
MLA_HEADS = 4
MLA_Q_RANK = 256
MLA_KV_RANK = 128
MLA_NOPE = 64
MLA_ROPE = 32
MLA_V = 64

N_GROUPS = 4
GROUP_W = 4 * HEAD_DIM
MIX_WIDTH = N_GROUPS * GROUP_W
IN_SIZES = (WIN_HEADS * HEAD_DIM, WIN_KV * HEAD_DIM, WIN_KV * HEAD_DIM,
            AX_HEADS * HEAD_DIM, AX_KV * HEAD_DIM, AX_KV * HEAD_DIM,
            DIL_HEADS * HEAD_DIM, DIL_KV * HEAD_DIM, DIL_KV * HEAD_DIM,
            MLA_Q_RANK, MLA_KV_RANK, MLA_ROPE)
IN_COLS = sum(IN_SIZES)

PEER_KEYS = 128
PEER_N = PEER_KEYS * PEER_KEYS
PEER_HEADS = 8
PEER_DK = 256
PEER_TOPK = 16
PEER_CHUNK = 128

kernel_name = "hybrid_parallel_heads_peer_encoder"

def rms_norm(x, g):
    xf = x.astype(jnp.float32)
    y = xf * lax.rsqrt(jnp.mean(xf * xf, axis=-1, keepdims=True) + EPS)
    return (y * g.astype(jnp.float32)).astype(x.dtype)

def rope_angles(pos, dim):
    inv = ROPE_THETA ** (-jnp.arange(0, dim, 2, dtype=jnp.float32) / dim)
    ang = pos.astype(jnp.float32)[:, None] * inv[None, :]
    return jnp.cos(ang), jnp.sin(ang)

def apply_rope(x, cos, sin):
    half = x.shape[-1] // 2
    xf = x.astype(jnp.float32)
    x1, x2 = xf[..., :half], xf[..., half:]
    c, s = cos[None, :, None, :], sin[None, :, None, :]
    return jnp.concatenate([x1 * c - x2 * s, x2 * c + x1 * s], axis=-1).astype(x.dtype)

def dense_attention_blocks(q, k, v, scale):
    b, s_len, kv, g, dk = q.shape
    nb = s_len // BLOCK
    qb = q.reshape(b, nb, BLOCK, kv, g, dk).transpose(1, 0, 2, 3, 4, 5)

    def one(qblk):
        sc = jnp.einsum('bqkgd,bskd->bkgqs', qblk, k, preferred_element_type=jnp.float32) * scale
        p = jax.nn.softmax(sc, axis=-1).astype(v.dtype)
        return jnp.einsum('bkgqs,bskd->bqkgd', p, v)

    o = lax.map(one, qb)
    return o.transpose(1, 0, 2, 3, 4, 5).reshape(b, s_len, kv, g, v.shape[-1])

def windowed_attention_sink(q, k, v, sink):
    b, s_len, kv, g, hd = q.shape
    nb = s_len // BLOCK
    qb = q.reshape(b, nb, BLOCK, kv, g, hd)

    def neighbours(t):
        tb = t.reshape(b, nb, BLOCK, kv, t.shape[-1])
        pad = jnp.zeros_like(tb[:, :1])
        tp = jnp.concatenate([pad, tb, pad], axis=1)
        return jnp.concatenate([tp[:, :-2], tp[:, 1:-1], tp[:, 2:]], axis=2)

    kw, vw = neighbours(k), neighbours(v)
    qpos = jnp.arange(nb)[:, None] * BLOCK + jnp.arange(BLOCK)[None, :]
    kpos = jnp.arange(nb)[:, None] * BLOCK + jnp.arange(-BLOCK, 2 * BLOCK)[None, :]
    rel = kpos[:, None, :] - qpos[:, :, None]
    valid = (jnp.abs(rel) <= WIN_RADIUS) & (kpos[:, None, :] >= 0) & (kpos[:, None, :] < s_len)
    sc = jnp.einsum('bnqkgd,bnskd->bnkgqs', qb, kw, preferred_element_type=jnp.float32) * (hd ** -0.5)
    sc = jnp.where(valid[None, :, None, None], sc, NEG)
    sink_l = sink.astype(jnp.float32).reshape(kv, g)[None, None, :, :, None, None]
    m = jnp.maximum(jnp.max(sc, axis=-1, keepdims=True), sink_l)
    e = jnp.exp(sc - m)
    p = (e / (jnp.sum(e, axis=-1, keepdims=True) + jnp.exp(sink_l - m))).astype(v.dtype)
    o = jnp.einsum('bnkgqs,bnskd->bnqkgd', p, vw)
    return o.reshape(b, s_len, kv, g, hd)

def dilated_attention(q, k, v):
    b, s_len, kv, g, hd = q.shape
    nb = s_len // BLOCK
    offs_np = np.stack([np.concatenate([-np.arange(w // 2, 0, -r), np.zeros(1, np.int64), np.arange(r, w // 2 + 1, r)])
                        for (w, r) in DIL_PATTERNS]).astype(np.int32)
    offs = jnp.asarray(offs_np)
    qb = q.reshape(b, nb, BLOCK, kv, g, hd).transpose(1, 0, 2, 3, 4, 5)

    def one(args):
        qblk, q0 = args
        qpos = q0 + jnp.arange(BLOCK)
        kpos = qpos[None, :, None] + offs[:, None, :]
        valid = (kpos >= 0) & (kpos < s_len)
        kidx = jnp.clip(kpos, 0, s_len - 1)
        kg = k[:, kidx]
        vg = v[:, kidx]
        sc = jnp.einsum('bqkgd,bpqjkd->bpkgqj', qblk, kg, preferred_element_type=jnp.float32) * (hd ** -0.5)
        sc = jnp.where(valid[None, :, None, None, :, :], sc, NEG)
        lse = jax.nn.logsumexp(sc, axis=-1)
        p = jnp.exp(sc - lse[..., None]).astype(v.dtype)
        o = jnp.einsum('bpkgqj,bpqjkd->bpqkgd', p, vg)
        wts = jax.nn.softmax(lse, axis=1).astype(o.dtype)
        return jnp.einsum('bpkgq,bpqkgd->bqkgd', wts, o)

    o = lax.map(one, (qb, jnp.arange(nb) * BLOCK))
    return o.transpose(1, 0, 2, 3, 4, 5).reshape(b, s_len, kv, g, hd)

def mixer_window(q, k, v, sink, cos, sin):
    b, s_len, _ = q.shape
    q = apply_rope(q.reshape(b, s_len, WIN_HEADS, HEAD_DIM), cos, sin).reshape(b, s_len, WIN_KV, WIN_HEADS // WIN_KV, HEAD_DIM)
    k = apply_rope(k.reshape(b, s_len, WIN_KV, HEAD_DIM), cos, sin)
    v = v.reshape(b, s_len, WIN_KV, HEAD_DIM)
    return windowed_attention_sink(q, k, v, sink).reshape(b, s_len, WIN_HEADS * HEAD_DIM)

def rope_2d(x, cos_r, sin_r, cos_c, sin_c):
    half = x.shape[-1] // 2
    return jnp.concatenate([apply_rope(x[..., :half], cos_r, sin_r), apply_rope(x[..., half:], cos_c, sin_c)], axis=-1)

def mixer_axial(q, k, v, g_qn, g_kn, cos_r, sin_r, cos_c, sin_c):
    b, s_len, _ = q.shape
    q = rope_2d(rms_norm(q.reshape(b, s_len, AX_HEADS, HEAD_DIM), g_qn), cos_r, sin_r, cos_c, sin_c)
    k = rope_2d(rms_norm(k.reshape(b, s_len, AX_KV, HEAD_DIM), g_kn), cos_r, sin_r, cos_c, sin_c)
    v = v.reshape(b, s_len, AX_KV, HEAD_DIM)
    q = q.reshape(b, s_len, AX_KV, AX_HEADS // AX_KV, HEAD_DIM)
    return dense_attention_blocks(q, k, v, HEAD_DIM ** -0.5).reshape(b, s_len, AX_HEADS * HEAD_DIM)

def mixer_dilated(q, k, v, cos, sin):
    b, s_len, _ = q.shape
    q = apply_rope(q.reshape(b, s_len, DIL_HEADS, HEAD_DIM), cos, sin).reshape(b, s_len, DIL_KV, DIL_HEADS // DIL_KV, HEAD_DIM)
    k = apply_rope(k.reshape(b, s_len, DIL_KV, HEAD_DIM), cos, sin)
    v = v.reshape(b, s_len, DIL_KV, HEAD_DIM)
    return dilated_attention(q, k, v).reshape(b, s_len, DIL_HEADS * HEAD_DIM)

def mixer_mla(c_q, c_kv, k_r, g_cq, g_ckv, w_uq, w_ukv, cos, sin):
    b, s_len, _ = c_q.shape
    q = (rms_norm(c_q, g_cq) @ w_uq).reshape(b, s_len, MLA_HEADS, MLA_NOPE + MLA_ROPE)
    q = jnp.concatenate([q[..., :MLA_NOPE], apply_rope(q[..., MLA_NOPE:], cos, sin)], axis=-1)
    kv = (rms_norm(c_kv, g_ckv) @ w_ukv).reshape(b, s_len, MLA_HEADS, MLA_NOPE + MLA_V)
    k_r = apply_rope(k_r[:, :, None, :], cos, sin)
    k = jnp.concatenate([kv[..., :MLA_NOPE], jnp.broadcast_to(k_r, (b, s_len, MLA_HEADS, MLA_ROPE))], axis=-1)
    v = kv[..., MLA_NOPE:]
    o = dense_attention_blocks(q[:, :, :, None, :], k, v, (MLA_NOPE + MLA_ROPE) ** -0.5)
    return o.reshape(b, s_len, MLA_HEADS * MLA_V)

def peer_ffn(h, w_q, sub_keys, u_tab, v_tab):
    b, s_len, d = h.shape
    t = b * s_len
    hf = h.reshape(t, d)
    qry = (hf @ w_q).reshape(t, PEER_HEADS, 2, PEER_DK // 2)
    sc = jnp.einsum('thcd,hcnd->thcn', qry, sub_keys, preferred_element_type=jnp.float32)
    s1, i1 = lax.top_k(sc[:, :, 0], PEER_TOPK)
    s2, i2 = lax.top_k(sc[:, :, 1], PEER_TOPK)
    cand = (s1[..., :, None] + s2[..., None, :]).reshape(t, PEER_HEADS, PEER_TOPK * PEER_TOPK)
    cidx = (i1[..., :, None] * PEER_KEYS + i2[..., None, :]).reshape(t, PEER_HEADS, PEER_TOPK * PEER_TOPK)
    best, sel = lax.top_k(cand, PEER_TOPK)
    eidx = jnp.take_along_axis(cidx, sel, axis=-1)
    gate = jax.nn.softmax(best, axis=-1)
    nc = t // PEER_CHUNK

    def one(args):
        xc, ec, gc = args
        u = jnp.take(u_tab, ec, axis=0)
        a = jax.nn.gelu(jnp.einsum('chkd,cd->chk', u, xc), approximate=False)
        wgt = gc.astype(a.dtype) * a
        vv = jnp.take(v_tab, ec, axis=0)
        return jnp.einsum('chk,chkd->cd', wgt, vv)

    out = lax.map(one, (hf.reshape(nc, PEER_CHUNK, d),
                        eidx.reshape(nc, PEER_CHUNK, PEER_HEADS, PEER_TOPK),
                        gate.reshape(nc, PEER_CHUNK, PEER_HEADS, PEER_TOPK)))
    return out.reshape(b, s_len, d)

def setup_inputs(seed: int = 0) -> dict:
    key = jax.random.key(seed)
    ks = jax.random.split(key, 18)
    f32 = jnp.float32

    def nrm(k, shape, scale):
        return jax.random.normal(k, shape, f32) * scale

    def gain(k, shape):
        return 1.0 + 0.05 * jax.random.normal(k, shape, f32)

    return {
        'x': nrm(ks[0], (BATCH, SEQ, D_MODEL), 1.0),
        'g_mix': gain(ks[1], (DEPTH, D_MODEL)),
        'w_in': nrm(ks[2], (DEPTH, D_MODEL, IN_COLS), D_MODEL ** -0.5),
        'win_sink': nrm(ks[3], (DEPTH, WIN_HEADS), 0.5),
        'ax_q_norm': gain(ks[4], (DEPTH, HEAD_DIM)),
        'ax_k_norm': gain(ks[5], (DEPTH, HEAD_DIM)),
        'mla_q_norm': gain(ks[6], (DEPTH, MLA_Q_RANK)),
        'mla_kv_norm': gain(ks[7], (DEPTH, MLA_KV_RANK)),
        'mla_w_uq': nrm(ks[8], (DEPTH, MLA_Q_RANK, MLA_HEADS * (MLA_NOPE + MLA_ROPE)), MLA_Q_RANK ** -0.5),
        'mla_w_ukv': nrm(ks[9], (DEPTH, MLA_KV_RANK, MLA_HEADS * (MLA_NOPE + MLA_V)), MLA_KV_RANK ** -0.5),
        'g_group': gain(ks[10], (DEPTH, N_GROUPS, GROUP_W)),
        'w_out': nrm(ks[11], (DEPTH, MIX_WIDTH, D_MODEL), MIX_WIDTH ** -0.5),
        'g_ffn': gain(ks[12], (DEPTH, D_MODEL)),
        'peer_w_q': nrm(ks[13], (DEPTH, D_MODEL, PEER_HEADS * PEER_DK), D_MODEL ** -0.5),
        'peer_sub_keys': nrm(ks[14], (DEPTH, PEER_HEADS, 2, PEER_KEYS, PEER_DK // 2), (PEER_DK // 2) ** -0.5),
        'peer_u': nrm(ks[15], (DEPTH, PEER_N, D_MODEL), D_MODEL ** -0.5),
        'peer_v': nrm(ks[16], (DEPTH, PEER_N, D_MODEL), PEER_HEADS ** -0.5),
        'g_final': gain(ks[17], (D_MODEL,)),
    }

def reference(x, g_mix, w_in, win_sink, ax_q_norm, ax_k_norm, mla_q_norm, mla_kv_norm, mla_w_uq, mla_w_ukv,
              g_group, w_out, g_ffn, peer_w_q, peer_sub_keys, peer_u, peer_v, g_final):
    b, s_len, _ = x.shape
    pos = jnp.arange(s_len)
    rows = s_len // GRID_W
    row = jnp.repeat(jnp.arange(rows), GRID_W)
    col = jnp.tile(jnp.arange(GRID_W), rows)
    cos1, sin1 = rope_angles(pos, HEAD_DIM)
    cos_m, sin_m = rope_angles(pos, MLA_ROPE)
    cos_r, sin_r = rope_angles(row, HEAD_DIM // 2)
    cos_c, sin_c = rope_angles(col, HEAD_DIM // 2)
    splits = np.cumsum(IN_SIZES)[:-1].tolist()
    for l in range(DEPTH):
        h = rms_norm(x, g_mix[l])
        z = h @ w_in[l]
        (aq, ak, av, bq, bk, bv, cq, ck, cv, dcq, dckv, dkr) = jnp.split(z, splits, axis=-1)
        o_a = mixer_window(aq, ak, av, win_sink[l], cos1, sin1)
        o_b = mixer_axial(bq, bk, bv, ax_q_norm[l], ax_k_norm[l], cos_r, sin_r, cos_c, sin_c)
        o_c = mixer_dilated(cq, ck, cv, cos1, sin1)
        o_d = mixer_mla(dcq, dckv, dkr, mla_q_norm[l], mla_kv_norm[l], mla_w_uq[l], mla_w_ukv[l], cos_m, sin_m)
        y = jnp.concatenate([rms_norm(o_a, g_group[l, 0]), rms_norm(o_b, g_group[l, 1]),
                             rms_norm(o_c, g_group[l, 2]), rms_norm(o_d, g_group[l, 3])], axis=-1)
        x = x + y @ w_out[l]
        x = x + peer_ffn(rms_norm(x, g_ffn[l]), peer_w_q[l], peer_sub_keys[l], peer_u[l], peer_v[l])
    return rms_norm(x, g_final)


_drawn_inputs = setup_inputs


def setup_inputs(seed=0):
    import zlib

    import numpy as np

    out = dict(_drawn_inputs(seed))
    spreads = {}
    factors = {'win_sink': 8.0}
    for name, (base, spread) in spreads.items():
        noise = np.random.default_rng([zlib.crc32(name.encode()), seed]).standard_normal(out[name].shape)
        drawn = base * np.exp(spread * noise) if base else spread * noise
        out[name] = __import__('jax').numpy.asarray(drawn.astype(out[name].dtype))
    for name, factor in factors.items():
        out[name] = (out[name] * factor).astype(out[name].dtype)
    return out
```

```python
from contextlib import ExitStack

import concourse.bass as bass
from concourse import mybir

ALU = mybir.AluOpType
ACT = mybir.ActivationFunctionType
AX = mybir.AxisListType
F32 = mybir.dt.float32
U32 = mybir.dt.uint32
I32 = mybir.dt.int32

P = 128
SEQ, D = 512, 1024
DEPTH = 2
NT = SEQ // P
KD = D // P
EPS = 1e-6
HD = 64
NH = 4
GROUP_W = NH * HD
ZW = 3 * 512 + 256 + 128 + 32
GRP = 512
Z_CQ, Z_CKV, Z_KR = 1536, 1792, 1920
QKH = 6
MQ = 96
ZCH, ZC = 4, ZW // 4
NEG = -1e30
LOWEST = -3.0e38

PH, PK, TOPK = 8, 128, 16
NEXP = PK * PK
HC = 2 * PH
SLOTS = PH * TOPK
R = 8
HALF = R // 2
UH = SLOTS // HALF
USES = 2 * SLOTS // R
PE_PER_HALF = 3
NDIAG = 6
PE_SLOTS = SLOTS * PE_PER_HALF // HALF
WQ_SLOTS = 12

HEADS = [(g, h) for g in (1, 3, 0, 2) for h in range(NH)]


def psum_jobs():
    jobs = []

    def two(kind, n, start=0):
        for i in range(n):
            jobs.append(((kind, i), "ACT" if (i + start) % 2 == 0 else "DVE"))

    two("hT", KD)
    two("z", ZCH * NT)
    two("cT", 3, 1)
    two("qu", NT)
    two("kv", NT)

    def qk(i):
        g, h = HEADS[i]
        jobs.append((("qT", i), "ACT"))
        if g == 3 or h % 2 == 0:
            jobs.append((("kT", i), "DVE"))

    qk(0)
    for i in range(len(HEADS)):
        if i + 1 < len(HEADS):
            qk(i + 1)
        for kt in range(NT):
            jobs.append((("pT", i, kt), "ACT" if kt % 2 else "DVE"))
        jobs.append((("o", i), "DVE"))
    two("yT", KD)
    for i in range(2 * NT):
        jobs.append((("out", i), "DVE"))
    two("hT2", KD)
    two("qry", HC)
    return jobs


JOBS = psum_jobs()
NJ = len(JOBS)
ENG = {name: e for name, e in JOBS}
INDEX = {name: i for i, (name, _) in enumerate(JOBS)}
ORD = {}
COUNT = {"ACT": 0, "DVE": 0}
for _name, _e in JOBS:
    ORD[_name] = COUNT[_e]
    COUNT[_e] += 1


def trunk(nc, x, w_in, w_out, w_q, w_uq, w_ukv, subk, peer_u, peer_v, g_mix, g_ffn, g_group, g_final, g_c, g_qk,
          sink, rope, rope_m, masks, out):
    with ExitStack() as ctx:
        def sb(name, shape, dt=F32):
            return ctx.enter_context(nc.sbuf_tensor(name, shape, dt))

        def sem(name):
            return ctx.enter_context(nc.semaphore(name))

        X = sb("X", [P, NT, D])
        H = sb("H", [P, NT, D])
        HT = sb("HT", [P, KD, SEQ])
        WB = sb("WB", [P, WQ_SLOTS * D])
        QRY = sb("QRY", [P, HC, SEQ])
        SH = sb("SH", [P, NT * ZW + 3 * NT * SEQ])
        GA = sb("GA", [P, D])
        GG = sb("GG", [P, D])
        GC = sb("GC", [P, 384])
        GQK = sb("GQK", [P, 2, HD])
        SK = sb("SK", [P, NH])
        ROPE = sb("ROPE", [P, 4, NT, HD])
        ROPM = sb("ROPM", [P, 2, NT, 32])
        ID = sb("ID", [P, P])
        IOTI = sb("IOTI", [P, TOPK], I32)
        IOT = sb("IOT", [P, TOPK])
        LOFF = sb("LOFF", [P, 1])
        TICK = sb("TICK", [P, 1])
        SS = sb("SS", [P, 32])
        RST = sb("RST", [P, 32])
        MX = sb("MX", [P, 2, NT])
        NM = sb("NM", [P, 2, NT])
        RS = sb("RS", [P, 2, NT])
        RI = sb("RI", [P, 2, NT])
        SE = sb("SE", [P, 2, NT])
        QT = sb("QT", [MQ, 2, SEQ])
        KT = sb("KT", [MQ, 2, SEQ])
        BK = ctx.enter_context(nc.psum_tensor("BK", [P, 8, 512], F32))

        hflat = H[:].rearrange("p t d -> p (t d)")
        QU_AT, KC_AT = 0, NT * NH * MQ
        QU = hflat[:, 0:NT * NH * MQ].rearrange("p (t n) -> p t n", t=NT)
        KC = hflat[:, NT * NH * MQ:2 * NT * NH * MQ].rearrange("p (t h n) -> p t h n", t=NT, h=NH)
        VD = hflat[:, 2 * NT * NH * MQ:2 * NT * NH * MQ + NT * GROUP_W].rearrange("p (t n) -> p t n", t=NT)
        scr = HT[:].rearrange("p k s -> p (k s)")
        SCR_D = scr[:, 0:NT * 384].rearrange("p (t n) -> p t n", t=NT)
        SCR_P = scr[:, 2048:2048 + NT * 384].rearrange("p (t n) -> p t n", t=NT)
        SQ = scr[:, 0:NT * NT * GROUP_W].rearrange("p (t g n) -> p t g n", t=NT, g=4)
        qflat = QRY[:].rearrange("p a s -> p (a s)")
        MASK = [qflat[:, i * 2048:(i + 1) * 2048].rearrange("p (t s) -> p t s", t=NT) for i in range(2)]
        WUQ = qflat[:, 4096:4096 + 768].rearrange("p (k n) -> p k n", k=2)
        WUKV = qflat[:, 4864:4864 + 512]
        Z = SH[:, 0:NT * ZW].rearrange("p (t n) -> p t n", t=NT)
        PR = SH[:, NT * ZW:NT * ZW + 4096].rearrange("p (b t s) -> p b t s", b=2, t=NT)
        PT = SH[:, NT * ZW + 4096:NT * ZW + 6144].rearrange("p (t s) -> p t s", t=NT)
        CT = PT[:, 0:3, :]
        place = [0]

        def shared(n):
            place[0] += n
            return SH[:, place[0] - n:place[0]]

        SUBK = shared(2048).rearrange("p (a n) -> p a n", a=HC)
        QST = shared(2048).rearrange("p (a n) -> p a n", a=HC)
        HCUR = shared(D)
        ACC = shared(D)
        DIAG = shared(NDIAG * P).rearrange("p (n m) -> p n m", n=NDIAG)
        S12 = shared(HC * TOPK).rearrange("p (a k) -> p a k", a=HC)
        I12 = shared(HC * TOPK).bitcast(U32).rearrange("p (a k) -> p a k", a=HC)
        I12F = shared(HC * TOPK).rearrange("p (a k) -> p a k", a=HC)
        SW = shared(2 * PK).rearrange("p (c n) -> p c n", c=2)
        CA, CB = shared(TOPK * TOPK), shared(TOPK * TOPK)
        BEST = shared(SLOTS).rearrange("p (h k) -> p h k", h=PH)
        POS = shared(SLOTS).bitcast(U32).rearrange("p (h k) -> p h k", h=PH)
        PAB = shared(2 * TOPK).bitcast(U32).rearrange("p (c k) -> p c k", c=2)
        PABF = shared(2 * TOPK).rearrange("p (c k) -> p c k", c=2)
        ONE = shared(2 * TOPK * TOPK).rearrange("p (c k a) -> p c k a", c=2, k=TOPK)
        ISEL = shared(2 * TOPK).rearrange("p (c k) -> p c k", c=2)
        EIDX = shared(SLOTS)
        IDXU, IDXV = shared(SLOTS).bitcast(I32), shared(SLOTS).bitcast(I32)
        GE = shared(SLOTS).rearrange("p (h k) -> p h k", h=PH)
        GATE = shared(SLOTS).rearrange("p (h k) -> p h k", h=PH)
        GSUM = shared(PH)
        ADOT = shared(SLOTS)
        AGELU = shared(SLOTS)
        WGT = shared(SLOTS)
        assert place[0] <= NT * ZW + 3 * NT * SEQ

        WZ = [WB[:, i * KD * ZC:(i + 1) * KD * ZC].rearrange("p (k n) -> p k n", k=KD) for i in range(3)]
        WO = WB[:, 0:KD * D].rearrange("p (k n) -> p k n", k=KD)
        WQ = [WB[:, i * D:(i + 1) * D].rearrange("p (k n) -> p k n", k=KD) for i in range(WQ_SLOTS)]
        RING = [WB[:, i * D:(i + 1) * D] for i in range(R)]
        SC = BK[:, 0:4, :].rearrange("p b (a n) -> p (b a) n", n=PK)
        YV = BK[:, 4:6, :].rearrange("p b n -> p (b n)")

        ld_x, ld_const = sem("ld_x"), sem("ld_const")
        ld_ga, ld_attn, ld_wo, ld_sub, ld_gf = sem("ld_ga"), sem("ld_attn"), sem("ld_wo"), sem("ld_sub"), sem("ld_gf")
        ld_wz = [sem(f"ld_wz{i}") for i in range(ZCH)]
        ld_wq = [sem(f"ld_wq{i}") for i in range(HC)]
        stored = sem("stored")
        ident_done, iota_done = sem("ident_done"), sem("iota_done")
        layer_open = sem("layer_open")
        psum_full = sem("psum_full")
        act_free, dve_free = sem("act_free"), sem("dve_free")
        act_sq, dve_var, act_rt = sem("act_sq"), sem("dve_var"), sem("act_rt")
        h_ready, c_ready = sem("h_ready"), sem("c_ready")
        qkd_ready, b_ready, ac_ready = sem("qkd_ready"), sem("b_ready"), sem("ac_ready")
        s_full, s_max, p_ready, sink_e, y_ready = sem("s_full"), sem("s_max"), sem("p_ready"), sem("sink_e"), sem("y_ready")
        q_staged, h_staged, sc_full, sc_used = sem("q_staged"), sem("h_staged"), sem("sc_full"), sem("sc_used")
        best_ready, ge_ready = sem("best_ready"), sem("ge_ready")
        idxu_ready, idxv_ready = sem("idxu_ready"), sem("idxv_ready")
        slot = [sem(f"slot{i}") for i in range(R)]
        used_dve, used_pe = sem("used_dve"), sem("used_pe")
        u_done, gelu_done, w_ready = sem("u_done"), sem("gelu_done"), sem("w_ready")
        diag_ready, v_done, v_taken = sem("diag_ready"), sem("v_done"), sem("v_taken")

        table_u = peer_u.rearrange("l n d -> (l n) d")
        table_v = peer_v.rearrange("l n d -> (l n) d")

        def bank(name):
            return 4 + INDEX[name] % 4

        def freed(eng, l, name):
            s = act_free if ENG[name] == "ACT" else dve_free
            eng.wait_ge(s, l * COUNT[ENG[name]] + ORD[name] + 1)

        def full(eng, l, name):
            eng.wait_ge(psum_full, l * NJ + INDEX[name] + 1)

        block = ctx.enter_context(nc.Block())

        @block.sync
        def _(sp):
            sp.dma_start(X[:], x[0].rearrange("(t p) d -> p t d", p=P)).then_inc(ld_x, 16)
            for i in range(4):
                sp.dma_start(ROPE[:, i], rope[i].rearrange("(t p) n -> p t n", p=P)).then_inc(ld_const, 16)
            for i in range(2):
                sp.dma_start(ROPM[:, i], rope_m[i].rearrange("(t p) n -> p t n", p=P)).then_inc(ld_const, 16)
            with sp.Fori(0, DEPTH) as l:
                sp.wait_ge(layer_open, l + 1)
                sp.dma_start(GA[:], g_mix[bass.ds(l, 1)].broadcast_to([P, D])).then_inc(ld_ga, 16)
                for c in range(3):
                    sp.dma_start(WB[:, c * KD * ZC:(c + 1) * KD * ZC], w_in[l, c]).then_inc(ld_wz[c], 16)
                sp.dma_start(GG[:], g_group[bass.ds(l, 1)].broadcast_to([P, D])).then_inc(ld_attn, 16)
                sp.dma_start(GC[:], g_c[bass.ds(l, 1)].broadcast_to([P, 384])).then_inc(ld_attn, 16)
                sp.dma_start(GQK[:].rearrange("p a n -> p (a n)"),
                             g_qk[bass.ds(l, 1)].broadcast_to([P, 2 * HD])).then_inc(ld_attn, 16)
                sp.dma_start(SK[:], sink[bass.ds(l, 1)].broadcast_to([P, NH])).then_inc(ld_attn, 16)
                for i in range(2):
                    sp.dma_start(MASK[i], masks[i].rearrange("(t p) s -> p t s", p=P)).then_inc(ld_attn, 16)
                sp.dma_start(qflat[:, 4096:4096 + 768], w_uq[l]).then_inc(ld_attn, 16)
                sp.dma_start(WUKV, w_ukv[l]).then_inc(ld_attn, 16)
                full(sp, l, ("z", NT - 1))
                sp.dma_start(WB[:, 0:KD * ZC], w_in[l, 3]).then_inc(ld_wz[3], 16)
                full(sp, l, ("z", ZCH * NT - 1))
                sp.dma_start(WB[:, 0:KD * D], w_out[l]).then_inc(ld_wo, 16)
                sp.wait_ge(h_ready, l * 2 * NT + NT)
                sp.dma_start(GA[:], g_ffn[bass.ds(l, 1)].broadcast_to([P, D])).then_inc(ld_ga, 16)
                for i in range(HC):
                    s = (i + 8) % WQ_SLOTS
                    if i == 4:
                        full(sp, l, ("out", 2 * NT - 1))
                        sp.dma_start(SH[:, 0:HC * PK], subk[l]).then_inc(ld_sub, 16)
                    if i >= WQ_SLOTS:
                        full(sp, l, ("qry", i - WQ_SLOTS))
                    sp.dma_start(WB[:, s * D:(s + 1) * D], w_q[l, i]).then_inc(ld_wq[i], 16)
            sp.wait_ge(layer_open, DEPTH + 1)
            sp.dma_start(GA[:], g_final.broadcast_to([P, D])).then_inc(ld_gf, 16)
            for t in range(NT):
                sp.wait_ge(h_ready, DEPTH * 2 * NT + t + 1)
                sp.dma_start(out[0, t * P:(t + 1) * P, :], H[:, t, :]).then_inc(stored, 16)
            sp.wait_ge(stored, 16 * NT)

        @block.gpsimd
        def _(pool):
            dve_need, pe_need = pool.alloc_register("dve_need"), pool.alloc_register("pe_need")
            u_need, v_need = pool.alloc_register("u_need"), pool.alloc_register("v_need")
            nc.gpsimd.memset(ID[:], 0.0)
            pool.drain()
            nc.gpsimd.affine_select(out=ID[:], in_=ID[:], compare_op=ALU.not_equal, fill=1.0, base=0,
                                    pattern=[[-1, P]], channel_multiplier=1).then_inc(ident_done, 1)
            nc.gpsimd.iota(IOTI[:], [[1, TOPK]], base=0, channel_multiplier=0).then_inc(iota_done, 1)
            pool.wait_ge(ld_const, 16 * 6)
            pool.reg_mov(dve_need, 1)
            pool.reg_mov(pe_need, PE_PER_HALF)
            pool.reg_mov(u_need, 1)
            pool.reg_mov(v_need, 1)
            with pool.Fori(0, DEPTH) as l:
                freed(pool, l, ("z", ZCH * NT - 2))
                freed(pool, l, ("z", ZCH * NT - 1))
                for g in (0, 2):
                    zz = Z[:, :, g * GRP:g * GRP + QKH * HD].rearrange("p t (h n) -> p t h n", n=HD)
                    sc = SCR_P.rearrange("p t (h n) -> p t h n", n=HD)
                    cos = ROPE[:, 0].unsqueeze(2).broadcast_to([P, NT, QKH, HD])
                    sin = ROPE[:, 1].unsqueeze(2).broadcast_to([P, NT, QKH, HD])
                    nc.gpsimd.tensor_tensor(sc[:, :, :, 0:32], zz[:, :, :, 32:64], sin[:, :, :, 0:32], ALU.mult)
                    nc.gpsimd.tensor_tensor(sc[:, :, :, 32:64], zz[:, :, :, 0:32], sin[:, :, :, 32:64], ALU.mult)
                    pool.drain()
                    nc.gpsimd.tensor_tensor(zz, zz, cos, ALU.mult)
                    pool.drain()
                    nc.gpsimd.tensor_tensor(zz, zz, sc, ALU.add).then_inc(ac_ready, 1)
                    pool.drain()

                def ring_free(k):
                    v_before = k < 2 or k >= UH + 2
                    pool.wait_ge(used_dve, dve_need)
                    pool.reg_add(dve_need, dve_need, HALF if 1 <= k <= UH else 1)
                    if v_before:
                        pool.wait_ge(used_pe, pe_need)
                        pool.reg_add(pe_need, pe_need, PE_PER_HALF)

                def gather(table, idx, s):
                    nc.gpsimd.indirect_dma_start(
                        out=RING[s % R], out_offset=None, in_=table,
                        in_offset=bass.IndirectOffsetOnAxis(ap=idx[:, s:s + 1], axis=0)).then_inc(slot[s % R], 16)

                with pool.Fori(0, NT) as t:
                    pool.wait_ge(idxu_ready, u_need)
                    pool.reg_add(u_need, u_need, 1)
                    for s in range(SLOTS):
                        if s % HALF == 0:
                            ring_free(s // HALF)
                        gather(table_u, IDXU, s)
                    pool.wait_ge(idxv_ready, v_need)
                    pool.reg_add(v_need, v_need, 1)
                    for s in range(SLOTS):
                        if s % HALF == 0:
                            ring_free(UH + s // HALF)
                        gather(table_v, IDXV, s)
                pool.reg_add(u_need, u_need, 1)

        @block.tensor
        def _(pe):
            pe.wait_ge(ident_done, 1)
            pe.wait_ge(ld_const, 16 * 6)
            with pe.Fori(0, DEPTH) as l:
                def begin(name):
                    i = INDEX[name]
                    if i >= 4:
                        freed(pe, l, JOBS[i - 4][0])
                    return BK[:, bank(name), :]

                def transpose_tokens(kind, src, ready):
                    for k in range(KD):
                        b = begin((kind, k))
                        for t in range(NT):
                            if k == 0:
                                ready(t)
                            ins = nc.tensor.transpose(b[:, t * P:(t + 1) * P], src(t, k), ID[:])
                        ins.then_inc(psum_full, 1)

                def transposed(kind):
                    freed(pe, l, (kind, KD - 2))
                    freed(pe, l, (kind, KD - 1))

                transpose_tokens("hT", lambda t, k: H[:, t, k * P:(k + 1) * P],
                                 lambda t: pe.wait_ge(h_ready, l * 2 * NT + t + 1))
                transposed("hT")
                for c in range(ZCH):
                    pe.wait_ge(ld_wz[c], (l + 1) * 16)
                    for t in range(NT):
                        name = ("z", c * NT + t)
                        b = begin(name)
                        for k in range(KD):
                            ins = nc.tensor.matmul(b[:, 0:ZC], HT[:, k, t * P:(t + 1) * P], WZ[c % 3][:, k, :],
                                                   start=(k == 0), stop=(k == KD - 1))
                        ins.then_inc(psum_full, 1)
                pe.wait_ge(c_ready, l + 1)
                pe.wait_ge(ld_attn, (l + 1) * 16 * 8)
                for k in range(3):
                    b = begin(("cT", k))
                    for t in range(NT):
                        ins = nc.tensor.transpose(b[:, t * P:(t + 1) * P],
                                                  Z[:, t, Z_CQ + k * P:Z_CQ + (k + 1) * P], ID[:])
                    ins.then_inc(psum_full, 1)
                freed(pe, l, ("cT", 1))
                freed(pe, l, ("cT", 2))
                for t in range(NT):
                    b = begin(("qu", t))
                    for k in range(2):
                        ins = nc.tensor.matmul(b[:, 0:NH * MQ], CT[:, k, t * P:(t + 1) * P], WUQ[:, k, :],
                                               start=(k == 0), stop=(k == 1))
                    ins.then_inc(psum_full, 1)
                for t in range(NT):
                    b = begin(("kv", t))
                    nc.tensor.matmul(b, CT[:, 2, t * P:(t + 1) * P], WUKV, start=True, stop=True).then_inc(psum_full, 1)

                def queries(i):
                    g, h = HEADS[i]
                    if h == 0:
                        if g == 1:
                            pe.wait_ge(b_ready, l + 1)
                        elif g == 3:
                            pe.wait_ge(qkd_ready, l + 1)
                        else:
                            pe.wait_ge(ac_ready, l * 2 + (1 if g == 0 else 2))
                    b = begin(("qT", i))
                    for t in range(NT):
                        q = QU_AT + (t * NH + h) * MQ
                        src = hflat[:, q:q + P] if g == 3 else Z[:, t, g * GRP + h * HD:g * GRP + h * HD + P]
                        ins = nc.tensor.transpose(b[:, t * P:(t + 1) * P], src, ID[:])
                    ins.then_inc(psum_full, 1)
                    if ("kT", i) in INDEX:
                        b = begin(("kT", i))
                        for t in range(NT):
                            c = g * GRP + GROUP_W + h // 2 * HD
                            k = KC_AT + (t * NH + h) * MQ
                            src = hflat[:, k:k + P] if g == 3 else Z[:, t, c:c + P]
                            ins = nc.tensor.transpose(b[:, t * P:(t + 1) * P], src, ID[:])
                        ins.then_inc(psum_full, 1)

                def kt_buffer(i):
                    g, h = HEADS[i]
                    return h % 2 if g == 3 else (h // 2) % 2

                def scores(i):
                    g, h = HEADS[i]
                    w = MQ if g == 3 else HD
                    freed(pe, l, ("qT", i))
                    if ("kT", i) in INDEX:
                        freed(pe, l, ("kT", i))
                    if i > 0:
                        if HEADS[i - 1][0] in (0, 2):
                            pe.wait_ge(s_max, l * len(HEADS) + i)
                        else:
                            pe.wait_ge(p_ready, l * len(HEADS) + i)
                    for t in range(NT):
                        ins = nc.tensor.matmul(BK[:, t, :], QT[0:w, i % 2, t * P:(t + 1) * P],
                                               KT[0:w, kt_buffer(i), :], start=True, stop=True)
                    ins.then_inc(s_full, 1)

                def product(i):
                    g, h = HEADS[i]
                    pe.wait_ge(p_ready, l * len(HEADS) + i + 1)
                    for kt in range(NT):
                        b = begin(("pT", i, kt))
                        for t in range(NT):
                            ins = nc.tensor.transpose(b[:, t * P:(t + 1) * P], PR[:, i % 2, t, kt * P:(kt + 1) * P], ID[:])
                        ins.then_inc(psum_full, 1)
                    b = begin(("o", i))
                    freed(pe, l, ("pT", i, 2))
                    freed(pe, l, ("pT", i, 3))
                    for t in range(NT):
                        for kt in range(NT):
                            c = g * GRP + GROUP_W + 2 * HD + h // 2 * HD
                            v = VD[:, kt, h * HD:(h + 1) * HD] if g == 3 else Z[:, kt, c:c + HD]
                            ins = nc.tensor.matmul(b[:, t * HD:(t + 1) * HD], PT[:, kt, t * P:(t + 1) * P], v,
                                                   start=(kt == 0), stop=(kt == NT - 1))
                    ins.then_inc(psum_full, 1)

                queries(0)
                scores(0)
                for i in range(len(HEADS)):
                    if i + 1 < len(HEADS):
                        queries(i + 1)
                        scores(i + 1)
                    product(i)

                transpose_tokens("yT", lambda t, k: Z[:, t, k // 2 * GRP + k % 2 * P:k // 2 * GRP + k % 2 * P + P],
                                 lambda t: pe.wait_ge(y_ready, l + 1) if t == 0 else None)
                transposed("yT")
                pe.wait_ge(ld_wo, (l + 1) * 16)
                for t in range(NT):
                    for n in range(2):
                        b = begin(("out", 2 * t + n))
                        for k in range(KD):
                            ins = nc.tensor.matmul(b, HT[:, k, t * P:(t + 1) * P], WO[:, k, n * 512:(n + 1) * 512],
                                                   start=(k == 0), stop=(k == KD - 1))
                        ins.then_inc(psum_full, 1)

                transpose_tokens("hT2", lambda t, k: H[:, t, k * P:(k + 1) * P],
                                 lambda t: pe.wait_ge(h_ready, l * 2 * NT + NT + t + 1))
                transposed("hT2")
                for i in range(HC):
                    pe.wait_ge(ld_wq[i], (l + 1) * 16)
                    b = begin(("qry", i))
                    for k in range(KD):
                        ins = nc.tensor.matmul(b, WQ[(i + 8) % WQ_SLOTS][:, k, :], HT[:, k, :],
                                               start=(k == 0), stop=(k == KD - 1))
                    ins.then_inc(psum_full, 1)

                def key_scores(n):
                    pe.wait_ge(q_staged, l * (NT + 1) + n + 1)
                    for a in range(HC):
                        ins = nc.tensor.matmul(SC[:, a, :], QST[:, a, :], SUBK[:, a, :], start=True, stop=True)
                    ins.then_inc(sc_full, 1)

                pe.wait_ge(ld_sub, (l + 1) * 16)
                for i in range(4):
                    freed(pe, l, ("qry", HC - 1 - i))
                key_scores(0)
                with pe.Fori(0, NT) as t:
                    T = pe.snap(l * NT + t)
                    pe.wait_ge(sc_used, l * (NT + 1) + t + 1)
                    key_scores(t + 1)
                    rows = pe.snap(T * (USES * 16))
                    diags = pe.snap(T * PE_SLOTS)
                    pe.wait_ge(v_taken, T + 1)
                    n = 0
                    for s in range(SLOTS):
                        if s % HALF == HALF - 1:
                            continue
                        pe.wait_ge(diag_ready, diags + (n + 1))
                        pe.wait_ge(slot[s % R], rows + (SLOTS // R + s // R + 1) * 16)
                        for b in range(2):
                            ins = nc.tensor.matmul(BK[:, 4 + b, :], DIAG[:, n % NDIAG, :],
                                                   RING[s % R][:, b * 512:(b + 1) * 512],
                                                   start=(n == 0), stop=(n == PE_SLOTS - 1))
                        ins.then_inc(used_pe, 1)
                        n += 1

        @block.scalar
        def _(act):
            def copy_out(l, name, dst, src):
                full(act, l, name)
                nc.scalar.copy(dst, src).then_inc(act_free, 1)

            def square_sums(l, n):
                for t in range(NT):
                    nc.scalar.activation(H[:, t, :], X[:, t, :], ACT.Square, accum_out=SS[:, t:t + 1]).then_inc(act_sq, 1)

            def root(l, n, cols):
                act.wait_ge(dve_var, l * 4 + n + 1)
                nc.scalar.activation(RST[:, 0:cols], SS[:, 0:cols], ACT.Sqrt).then_inc(act_rt, 1)

            act.wait_ge(ld_x, 16)
            act.wait_ge(ident_done, 1)
            with act.Fori(0, DEPTH) as l:
                act.wait_ge(layer_open, l + 1)
                square_sums(l, 0)
                root(l, 0, NT)
                for k in range(0, KD, 2):
                    copy_out(l, ("hT", k), HT[:, k, :], BK[:, bank(("hT", k)), :])
                for i in range(0, ZCH * NT, 2):
                    c, t = i // NT, i % NT
                    copy_out(l, ("z", i), Z[:, t, c * ZC:(c + 1) * ZC], BK[:, bank(("z", i)), 0:ZC])
                root(l, 1, 32)
                copy_out(l, ("cT", 1), CT[:, 1, :], BK[:, bank(("cT", 1)), :])
                for t in range(0, NT, 2):
                    copy_out(l, ("qu", t), QU[:, t, :], BK[:, bank(("qu", t)), 0:NH * MQ])
                for t in range(0, NT, 2):
                    kv = BK[:, bank(("kv", t)), :].rearrange("p (h n) -> p h n", h=NH)
                    full(act, l, ("kv", t))
                    nc.scalar.copy(KC[:, t, :, 0:HD], kv[:, :, 0:HD])
                    nc.scalar.copy(VD[:, t, :].rearrange("p (h n) -> p h n", h=NH), kv[:, :, HD:2 * HD]).then_inc(act_free, 1)

                def queries(i):
                    w = MQ if HEADS[i][0] == 3 else HD
                    copy_out(l, ("qT", i), QT[0:w, i % 2, :], BK[0:w, bank(("qT", i)), :])

                def probs(i):
                    g, h = HEADS[i]
                    act.wait_ge(s_max, l * len(HEADS) + i + 1)
                    if i >= 2:
                        full(act, l, ("pT", i - 2, 3))
                    for t in range(NT):
                        bias = NM[:, i % 2, t:t + 1]
                        rows = RS[:, i % 2, t:t + 1]
                        if g in (0, 2):
                            ins = nc.scalar.activation(PR[:, i % 2, t, :], PR[:, i % 2, t, :], ACT.Exp, bias=bias,
                                                       accum_out=rows)
                        else:
                            ins = nc.scalar.activation(PR[:, i % 2, t, :], BK[:, t, :], ACT.Exp, bias=bias,
                                                       scale=(MQ if g == 3 else HD) ** -0.5, accum_out=rows)
                    if g == 0:
                        ins = nc.scalar.activation(SE[:, i % 2, :], NM[:, i % 2, :], ACT.Exp, bias=SK[:, h:h + 1])
                    ins.then_inc(p_ready, 1)

                act.wait_ge(ld_attn, (l + 1) * 16 * 8)
                queries(0)
                probs(0)
                for i in range(len(HEADS)):
                    if i + 1 < len(HEADS):
                        queries(i + 1)
                        probs(i + 1)
                    for kt in (1, 3):
                        copy_out(l, ("pT", i, kt), PT[:, kt, :], BK[:, bank(("pT", i, kt)), :])
                freed(act, l, ("o", len(HEADS) - 1))
                for g in range(4):
                    ins = nc.scalar.activation(SQ[:, :, g, :], Z[:, :, g * GRP:g * GRP + GROUP_W], ACT.Square)
                ins.then_inc(act_sq, 1)
                root(l, 2, 16)
                for k in range(0, KD, 2):
                    copy_out(l, ("yT", k), HT[:, k, :], BK[:, bank(("yT", k)), :])
                freed(act, l, ("out", 2 * NT - 1))
                square_sums(l, 1)
                root(l, 3, NT)
                for k in range(0, KD, 2):
                    copy_out(l, ("hT2", k), HT[:, k, :], BK[:, bank(("hT2", k)), :])
                for i in range(0, HC, 2):
                    copy_out(l, ("qry", i), QRY[:, i, :], BK[:, bank(("qry", i)), :])

                act.drain()
                freed(act, l, ("qry", HC - 1))
                act.wait_ge(h_ready, (l + 1) * 2 * NT)
                nc.scalar.copy(QST, QRY[:, :, 0:P]).then_inc(q_staged, 1)
                nc.scalar.copy(HCUR, H[:, 0, :]).then_inc(h_staged, 1)
                act.wait_ge(best_ready, l * (NT + 1) + 1)
                nc.scalar.activation(GE, GE, ACT.Exp).then_inc(ge_ready, 1)
                with act.Fori(0, NT) as t:
                    T = act.snap(l * NT + t)
                    nxt = act.snap((t + 1) % NT)
                    act.wait_ge(sc_full, l * (NT + 1) + t + 1)
                    nc.scalar.copy(QST, QRY[:, :, bass.ds(nxt * P, P)]).then_inc(q_staged, 1)
                    act.wait_ge(u_done, T + 1)
                    nc.scalar.activation(AGELU, ADOT, ACT.Gelu).then_inc(gelu_done, 1)
                    nc.scalar.copy(HCUR, H[:, bass.ds(nxt, 1), :].rearrange("p a d -> p (a d)")).then_inc(h_staged, 1)
                    used = act.snap(T * PE_SLOTS + PE_PER_HALF * 2)
                    act.wait_ge(w_ready, T + 1)
                    n = 0
                    for s in range(SLOTS):
                        if s % HALF == HALF - 1:
                            continue
                        if n % PE_PER_HALF == 0:
                            act.wait_ge(used_pe, used + (n - NDIAG + PE_PER_HALF))
                        nc.scalar.activation(DIAG[:, n % NDIAG, :], ID[:], ACT.Copy,
                                             scale=WGT[:, s:s + 1]).then_inc(diag_ready, 1)
                        n += 1
                    act.wait_ge(best_ready, l * (NT + 1) + t + 2)
                    nc.scalar.activation(GE, GE, ACT.Exp).then_inc(ge_ready, 1)
            act.wait_ge(layer_open, DEPTH + 1)
            square_sums(DEPTH, 0)
            act.wait_ge(dve_var, DEPTH * 4 + 1)
            nc.scalar.activation(RST[:, 0:NT], SS[:, 0:NT], ACT.Sqrt).then_inc(act_rt, 1)

        @block.vector
        def _(dve):
            v = nc.vector

            def arrived():
                v.tensor_copy(TICK[:], LOFF[:])
                dve.drain()

            def copy_out(l, name, dst, src):
                full(dve, l, name)
                v.tensor_copy(dst, src).then_inc(dve_free, 1)

            def rstd(l, n, widths):
                at = 0
                for cols, width in widths:
                    ins = v.tensor_scalar(SS[:, at:at + cols], SS[:, at:at + cols], 1.0 / width, EPS, ALU.mult, ALU.add)
                    at += cols
                ins.then_inc(dve_var, 1)
                dve.wait_ge(act_rt, l * 4 + n + 1)
                v.reciprocal(RST[:, 0:at], RST[:, 0:at])
                dve.drain()

            def normalise(l, n, squares):
                dve.wait_ge(act_sq, l * (2 * NT + 1) + squares + NT)
                rstd(l, n, [(NT, D)])
                for t in range(NT):
                    v.scalar_tensor_tensor(H[:, t, :], X[:, t, :], RST[:, t:t + 1], GA[:], ALU.mult, ALU.mult)\
                        .then_inc(h_ready, 1)

            v.memset(LOFF[:], 0.0)
            v.memset(MX[:], 0.0).then_inc(used_dve, 2)
            v.memset(NM[:], 0.0).then_inc(used_pe, 2 * PE_PER_HALF)
            v.memset(RI[:], 0.0).then_inc(v_taken, 1)
            v.memset(SS[:], 0.0).then_inc(layer_open, 1)
            dve.wait_ge(iota_done, 1)
            v.tensor_copy(IOT[:], IOTI[:])
            dve.wait_ge(ld_x, 16)
            dve.wait_ge(ld_const, 16 * 6)
            dve.drain()
            with dve.Fori(0, DEPTH) as l:
                dve.wait_ge(ld_ga, l * 32 + 16)
                normalise(l, 0, 0)
                for k in range(1, KD, 2):
                    copy_out(l, ("hT", k), HT[:, k, :], BK[:, bank(("hT", k)), :])
                for i in range(1, ZCH * NT, 2):
                    c, t = i // NT, i % NT
                    copy_out(l, ("z", i), Z[:, t, c * ZC:(c + 1) * ZC], BK[:, bank(("z", i)), 0:ZC])
                dve.drain()
                dve.wait_ge(ld_attn, (l + 1) * 16 * 8)
                freed(dve, l, ("z", ZCH * NT - 2))

                zb = Z[:, :, GRP:GRP + QKH * HD]
                zbh = zb.rearrange("p t (h n) -> p t h n", n=HD)
                zc = Z[:, :, Z_CQ:Z_CQ + 384]
                sh = SCR_D.rearrange("p t (h n) -> p t h n", n=HD)
                v.tensor_tensor(SCR_D, zb, zb, ALU.mult)
                dve.drain()
                v.tensor_reduce(SS[:, 0:24].rearrange("p (t h) -> p t h", t=NT), sh, AX.X, ALU.add)
                dve.drain()
                v.tensor_tensor(SCR_D, zc, zc, ALU.mult)
                dve.drain()
                v.tensor_reduce(SS[:, 24:28], SCR_D[:, :, 0:256], AX.X, ALU.add)
                v.tensor_reduce(SS[:, 28:32], SCR_D[:, :, 256:384], AX.X, ALU.add)
                dve.drain()
                rstd(l, 1, [(24, HD), (4, 256), (4, 128)])
                for t in range(NT):
                    v.scalar_tensor_tensor(Z[:, t, Z_CQ:Z_CQ + 256], Z[:, t, Z_CQ:Z_CQ + 256], RST[:, 24 + t:25 + t],
                                           GC[:, 0:256], ALU.mult, ALU.mult)
                    ins = v.scalar_tensor_tensor(Z[:, t, Z_CKV:Z_CKV + 128], Z[:, t, Z_CKV:Z_CKV + 128],
                                                 RST[:, 28 + t:29 + t], GC[:, 256:384], ALU.mult, ALU.mult)
                ins.then_inc(c_ready, 1)
                rb = RST[:, 0:24].rearrange("p (t h) -> p t h", t=NT).unsqueeze(3).broadcast_to([P, NT, QKH, HD])
                v.tensor_tensor(zbh, zbh, rb, ALU.mult)
                dve.drain()
                for a, (h0, h1) in enumerate(((0, NH), (NH, QKH))):
                    gain = GQK[:, a, :].unsqueeze(1).unsqueeze(1).broadcast_to([P, NT, h1 - h0, HD])
                    v.tensor_tensor(zbh[:, :, h0:h1, :], zbh[:, :, h0:h1, :], gain, ALU.mult)
                dve.drain()
                for r in range(2):
                    for a, b in ((0, 16), (16, 0)):
                        o, i = 32 * r + a, 32 * r + b
                        v.tensor_tensor(sh[:, :, :, o:o + 16], zbh[:, :, :, i:i + 16],
                                        ROPE[:, 3, :, o:o + 16].unsqueeze(2).broadcast_to([P, NT, QKH, 16]), ALU.mult)
                dve.drain()
                v.tensor_tensor(zbh, zbh, ROPE[:, 2].unsqueeze(2).broadcast_to([P, NT, QKH, HD]), ALU.mult)
                dve.drain()
                v.tensor_tensor(zbh, zbh, sh, ALU.add).then_inc(b_ready, 1)
                dve.drain()

                for k in (0, 2):
                    copy_out(l, ("cT", k), CT[:, k, :], BK[:, bank(("cT", k)), :])
                for t in range(1, NT, 2):
                    copy_out(l, ("qu", t), QU[:, t, :], BK[:, bank(("qu", t)), 0:NH * MQ])
                for t in range(1, NT, 2):
                    kv = BK[:, bank(("kv", t)), :].rearrange("p (h n) -> p h n", h=NH)
                    full(dve, l, ("kv", t))
                    v.tensor_copy(KC[:, t, :, 0:HD], kv[:, :, 0:HD])
                    v.tensor_copy(VD[:, t, :].rearrange("p (h n) -> p h n", h=NH), kv[:, :, HD:2 * HD]).then_inc(dve_free, 1)
                dve.drain()
                freed(dve, l, ("kv", NT - 2))
                qr = QU.rearrange("p t (h n) -> p t h n", n=MQ)
                kr = Z[:, :, Z_KR:Z_KR + 32]
                sq = SCR_D[:, :, 0:128].rearrange("p t (h n) -> p t h n", n=32)
                sk = SCR_D[:, :, 128:160]
                for a, b in ((0, 16), (16, 0)):
                    v.tensor_tensor(sq[:, :, :, a:a + 16], qr[:, :, :, 64 + b:80 + b],
                                    ROPM[:, 1, :, a:a + 16].unsqueeze(2).broadcast_to([P, NT, NH, 16]), ALU.mult)
                    v.tensor_tensor(sk[:, :, a:a + 16], kr[:, :, b:b + 16], ROPM[:, 1, :, a:a + 16], ALU.mult)
                dve.drain()
                v.tensor_tensor(qr[:, :, :, 64:96], qr[:, :, :, 64:96],
                                ROPM[:, 0].unsqueeze(2).broadcast_to([P, NT, NH, 32]), ALU.mult)
                v.tensor_tensor(kr, kr, ROPM[:, 0], ALU.mult)
                dve.drain()
                v.tensor_tensor(qr[:, :, :, 64:96], qr[:, :, :, 64:96], sq, ALU.add)
                for h in range(NH):
                    ins = v.tensor_tensor(KC[:, :, h, HD:MQ], kr, sk, ALU.add)
                ins.then_inc(qkd_ready, 1)

                def keys(i):
                    if ("kT", i) in INDEX:
                        g, h = HEADS[i]
                        w = MQ if g == 3 else HD
                        buf = h % 2 if g == 3 else (h // 2) % 2
                        copy_out(l, ("kT", i), KT[0:w, buf, :], BK[0:w, bank(("kT", i)), :])

                def maxima(i):
                    g, h = HEADS[i]
                    if i >= 2:
                        full(dve, l, ("pT", i - 2, 3))
                    dve.wait_ge(s_full, l * len(HEADS) + i + 1)
                    if g in (0, 2):
                        arrived()
                        for t in range(NT):
                            v.tensor_tensor_reduce(out=PR[:, i % 2, t, :], in0=BK[:, t, :], in1=MASK[g // 2][:, t, :],
                                                   scale=HD ** -0.5, scalar=LOWEST, op0=ALU.add, op1=ALU.max,
                                                   accum_out=MX[:, i % 2, t:t + 1])
                    else:
                        v.tensor_reduce(MX[:, i % 2, :], BK[:, 0:NT, :], AX.X, ALU.max)
                    dve.drain()
                    if g == 0:
                        v.tensor_scalar(NM[:, i % 2, :], MX[:, i % 2, :], SK[:, h:h + 1], -1.0, ALU.max, ALU.mult)\
                            .then_inc(s_max, 1)
                    else:
                        scale = -1.0 if g == 2 else -(MQ if g == 3 else HD) ** -0.5
                        v.tensor_scalar(NM[:, i % 2, :], MX[:, i % 2, :], scale, None, ALU.mult).then_inc(s_max, 1)

                keys(0)
                maxima(0)
                for i in range(len(HEADS)):
                    g, h = HEADS[i]
                    if i + 1 < len(HEADS):
                        keys(i + 1)
                        maxima(i + 1)
                    for kt in (0, 2):
                        copy_out(l, ("pT", i, kt), PT[:, kt, :], BK[:, bank(("pT", i, kt)), :])
                    dve.wait_ge(p_ready, l * len(HEADS) + i + 1)
                    if g == 0:
                        v.tensor_tensor(RS[:, i % 2, :], RS[:, i % 2, :], SE[:, i % 2, :], ALU.add)
                        dve.drain()
                    v.reciprocal(RI[:, i % 2, :], RS[:, i % 2, :])
                    dve.drain()
                    full(dve, l, ("o", i))
                    o = BK[:, bank(("o", i)), 0:NT * HD].rearrange("p (t n) -> p t n", t=NT)
                    v.tensor_tensor(Z[:, :, g * GRP + h * HD:g * GRP + (h + 1) * HD], o,
                                    RI[:, i % 2, :].unsqueeze(2).broadcast_to([P, NT, HD]), ALU.mult).then_inc(dve_free, 1)

                dve.wait_ge(act_sq, l * (2 * NT + 1) + NT + 1)
                v.tensor_reduce(SS[:, 0:16].rearrange("p (t g) -> p t g", t=NT), SQ, AX.X, ALU.add)
                dve.drain()
                rstd(l, 2, [(16, GROUP_W)])
                for t in range(NT):
                    for g in range(4):
                        zo = Z[:, t, g * GRP:g * GRP + GROUP_W]
                        ins = v.scalar_tensor_tensor(zo, zo, RST[:, 4 * t + g:4 * t + g + 1],
                                                     GG[:, g * GROUP_W:(g + 1) * GROUP_W], ALU.mult, ALU.mult)
                ins.then_inc(y_ready, 1)
                for k in range(1, KD, 2):
                    copy_out(l, ("yT", k), HT[:, k, :], BK[:, bank(("yT", k)), :])
                for t in range(NT):
                    for n in range(2):
                        name = ("out", 2 * t + n)
                        xs = X[:, t, n * 512:(n + 1) * 512]
                        full(dve, l, name)
                        v.tensor_tensor(xs, xs, BK[:, bank(name), :], ALU.add).then_inc(dve_free, 1)
                dve.wait_ge(ld_ga, (l + 1) * 32)
                normalise(l, 3, NT + 1)
                for k in range(1, KD, 2):
                    copy_out(l, ("hT2", k), HT[:, k, :], BK[:, bank(("hT2", k)), :])
                for i in range(1, HC, 2):
                    copy_out(l, ("qry", i), QRY[:, i, :], BK[:, bank(("qry", i)), :])

                def route_head(h):
                    two = range(2)
                    for c in two:
                        v.max(S12[:, 2 * h + c, 0:8], SC[:, 2 * h + c, :])
                    dve.drain()
                    for c in two:
                        v.max_index(I12[:, 2 * h + c, 0:8], S12[:, 2 * h + c, 0:8], SC[:, 2 * h + c, :])
                        v.match_replace(SW[:, c, :], S12[:, 2 * h + c, 0:8], SC[:, 2 * h + c, :], LOWEST)
                    dve.drain()
                    for c in two:
                        v.max(S12[:, 2 * h + c, 8:16], SW[:, c, :])
                    dve.drain()
                    for c in two:
                        v.max_index(I12[:, 2 * h + c, 8:16], S12[:, 2 * h + c, 8:16], SW[:, c, :])
                    v.tensor_tensor(CA.rearrange("p (a b) -> p a b", a=TOPK),
                                    S12[:, 2 * h, :].unsqueeze(2).broadcast_to([P, TOPK, TOPK]),
                                    S12[:, 2 * h + 1, :].unsqueeze(1).broadcast_to([P, TOPK, TOPK]), ALU.add)
                    dve.drain()
                    v.max(BEST[:, h, 0:8], CA)
                    v.tensor_copy(I12F[:, 2 * h:2 * h + 2, :], I12[:, 2 * h:2 * h + 2, :])
                    dve.drain()
                    v.max_index(POS[:, h, 0:8], BEST[:, h, 0:8], CA)
                    v.match_replace(CB, BEST[:, h, 0:8], CA, LOWEST)
                    dve.drain()
                    v.max(BEST[:, h, 8:16], CB)
                    dve.drain()
                    v.max_index(POS[:, h, 8:16], BEST[:, h, 8:16], CB)
                    dve.drain()
                    v.tensor_scalar(PAB[:, 0, :], POS[:, h, :], 4, None, ALU.logical_shift_right)
                    v.tensor_scalar(PAB[:, 1, :], POS[:, h, :], 15, None, ALU.bitwise_and)
                    dve.drain()
                    v.tensor_copy(PABF, PAB)
                    dve.drain()
                    for c in two:
                        v.tensor_tensor(ONE[:, c], IOT[:].unsqueeze(1).broadcast_to([P, TOPK, TOPK]),
                                        PABF[:, c, :].unsqueeze(2).broadcast_to([P, TOPK, TOPK]), ALU.is_equal)
                    dve.drain()
                    for c in two:
                        v.tensor_tensor(ONE[:, c], ONE[:, c],
                                        I12F[:, 2 * h + c, :].unsqueeze(1).broadcast_to([P, TOPK, TOPK]), ALU.mult)
                    dve.drain()
                    v.tensor_reduce(ISEL, ONE, AX.X, ALU.add)
                    dve.drain()
                    v.scalar_tensor_tensor(EIDX[:, h * TOPK:(h + 1) * TOPK], ISEL[:, 0, :], float(PK), ISEL[:, 1, :],
                                           ALU.mult, ALU.add)

                def route_end():
                    dve.drain()
                    v.tensor_scalar(IDXU, EIDX, LOFF[:, 0:1], None, ALU.add).then_inc(idxu_ready, 1)
                    v.tensor_tensor(GE, BEST, BEST[:, :, 0:1].broadcast_to([P, PH, TOPK]), ALU.subtract)\
                        .then_inc(best_ready, 1)

                def gates(n):
                    dve.wait_ge(ge_ready, l * (NT + 1) + n + 1)
                    v.tensor_reduce(GSUM, GE, AX.X, ALU.add)
                    dve.drain()
                    v.reciprocal(GSUM, GSUM)
                    dve.drain()
                    v.tensor_tensor(GATE, GE, GSUM.unsqueeze(2).broadcast_to([P, PH, TOPK]), ALU.mult)
                    dve.drain()

                dve.wait_ge(sc_full, l * (NT + 1) + 1)
                arrived()
                for h in range(PH):
                    route_head(h)
                dve.drain()
                v.tensor_copy(PABF, PAB).then_inc(sc_used, 1)
                route_end()
                v.tensor_scalar(IDXV, EIDX, LOFF[:, 0:1], None, ALU.add).then_inc(idxv_ready, 1)
                gates(0)
                with dve.Fori(0, NT) as t:
                    T = dve.snap(l * NT + t)
                    rows = dve.snap(T * (USES * 16))
                    dve.drain()
                    dve.wait_ge(h_staged, l * (NT + 1) + t + 1)
                    for s in range(SLOTS):
                        dve.wait_ge(slot[s % R], rows + (s // R + 1) * 16)
                        v.tensor_tensor_reduce(out=RING[s % R], in0=RING[s % R], in1=HCUR, scale=1.0, scalar=0.0,
                                               op0=ALU.mult, op1=ALU.add, accum_out=ADOT[:, s:s + 1]).then_inc(used_dve, 1)
                    dve.drain()
                    v.memset(ACC, 0.0).then_inc(u_done, 1)
                    dve.wait_ge(gelu_done, T + 1)
                    v.tensor_tensor(WGT, AGELU, GATE.rearrange("p h k -> p (h k)"), ALU.mult).then_inc(w_ready, 1)
                    for s in range(HALF - 1, SLOTS, HALF):
                        dve.drain()
                        dve.wait_ge(slot[s % R], rows + (SLOTS // R + s // R + 1) * 16)
                        v.scalar_tensor_tensor(ACC, RING[s % R], WGT[:, s:s + 1], ACC, ALU.mult, ALU.add)\
                            .then_inc(used_dve, 1)
                        k = s // HALF
                        if k == 0:
                            dve.wait_ge(sc_full, l * (NT + 1) + t + 2)
                            arrived()
                        if k % 3 == 1 and k // 3 < PH:
                            dve.drain()
                            route_head(k // 3)
                            if k // 3 == PH - 1:
                                dve.drain()
                                v.tensor_copy(PABF, PAB).then_inc(sc_used, 1)
                                route_end()
                    dve.drain()
                    dve.wait_ge(used_pe, T * PE_SLOTS + PE_SLOTS + 2 * PE_PER_HALF)
                    v.tensor_scalar(IDXV, EIDX, LOFF[:, 0:1], None, ALU.add).then_inc(idxv_ready, 1)
                    xt = X[:, bass.ds(t, 1), :].rearrange("p a d -> p (a d)")
                    v.tensor_tensor(ACC, ACC, YV, ALU.add).then_inc(v_taken, 1)
                    dve.drain()
                    v.tensor_tensor(xt, xt, ACC, ALU.add)
                    gates(t + 1)
                v.tensor_scalar(LOFF[:], LOFF[:], float(NEXP), None, ALU.add)
                dve.drain()
                v.memset(MX[:], 0.0).then_inc(layer_open, 1)
            dve.wait_ge(ld_gf, 16)
            dve.wait_ge(act_sq, DEPTH * (2 * NT + 1) + NT)
            v.tensor_scalar(SS[:, 0:NT], SS[:, 0:NT], 1.0 / D, EPS, ALU.mult, ALU.add).then_inc(dve_var, 1)
            dve.wait_ge(act_rt, DEPTH * 4 + 1)
            v.reciprocal(RST[:, 0:NT], RST[:, 0:NT])
            dve.drain()
            for t in range(NT):
                v.scalar_tensor_tensor(H[:, t, :], X[:, t, :], RST[:, t:t + 1], GA[:], ALU.mult, ALU.mult)\
                    .then_inc(h_ready, 1)


def shape_constants():
    import numpy as np
    f = np.float32

    def angles(pos, dim):
        inv = f(10000.0) ** (-np.arange(0, dim, 2, dtype=f) / f(dim))
        ang = pos.astype(f)[:, None] * inv[None, :].astype(f)
        return np.cos(ang).astype(f), np.sin(ang).astype(f)

    pos = np.arange(SEQ)
    c1, s1 = angles(pos, HD)
    cr, sr = angles(pos // 64, HD // 2)
    cc, sc = angles(pos % 64, HD // 2)
    cm, sm = angles(pos, 32)
    cat = lambda *a: np.concatenate(a, axis=1)
    rope = np.stack([cat(c1, c1), cat(-s1, s1), cat(cr, cr, cc, cc), cat(-sr, sr, -sc, sc)]).astype(f)
    rope_m = np.stack([cat(cm, cm), cat(-sm, sm)]).astype(f)
    rel = pos[None, :] - pos[:, None]
    window = np.where(np.abs(rel) <= 128, f(0), f(NEG))
    count = sum(((np.abs(rel) <= w // 2) & (rel % r == 0)).astype(int) for w, r in ((128, 1), (512, 4), (2048, 16)))
    dilated = np.where(count > 0, np.log(np.maximum(count, 1)) * HD ** 0.5, NEG)
    return rope, rope_m, np.stack([window, dilated]).astype(f)


def kernel(**inputs):
    import numpy as _np
    import concourse.bacc as _bacc
    from concourse import mybir as _mybir
    from concourse.bass_utils import run_bass_kernel_spmd as _run

    a = {k: _np.asarray(v) for k, v in inputs.items()}
    rope, rope_m, masks = shape_constants()

    def blocks(w, n):
        k = w.shape[1] // P
        return w.reshape(DEPTH, k, P, n, -1).transpose(0, 3, 2, 1, 4).reshape(DEPTH, n, P, -1)

    feeds = {
        "x": a["x"], "w_in": blocks(a["w_in"], ZCH), "w_out": blocks(a["w_out"], 1)[:, 0],
        "w_q": blocks(a["peer_w_q"], HC), "w_uq": blocks(a["mla_w_uq"], 1)[:, 0], "w_ukv": a["mla_w_ukv"],
        "subk": a["peer_sub_keys"].reshape(DEPTH, HC, PK, P).transpose(0, 3, 1, 2).reshape(DEPTH, P, HC * PK),
        "peer_u": a["peer_u"], "peer_v": a["peer_v"], "g_mix": a["g_mix"], "g_ffn": a["g_ffn"],
        "g_group": a["g_group"].reshape(DEPTH, D), "g_final": a["g_final"].reshape(1, D),
        "g_c": _np.concatenate([a["mla_q_norm"], a["mla_kv_norm"]], axis=1),
        "g_qk": _np.concatenate([a["ax_q_norm"], a["ax_k_norm"]], axis=1),
        "sink": a["win_sink"], "rope": rope, "rope_m": rope_m, "masks": masks,
    }
    nc = _bacc.Bacc("TRN2", target_bir_lowering=False, num_devices=1)
    arrays, args = {}, []
    for name, value in feeds.items():
        value = _np.ascontiguousarray(value)
        arrays[f"in_{name}_dram"] = value
        args.append(nc.dram_tensor(f"in_{name}_dram", value.shape, _mybir.dt.from_np(value.dtype),
                                   kind="ExternalInput").ap())
    out = nc.dram_tensor("out_0_dram", (1, SEQ, D), _mybir.dt.float32, kind="ExternalOutput").ap()
    trunk(nc, *args, out)
    r = _run(nc, [arrays], core_ids=[0])
    return r.results[0]["out_0_dram"]
```

```python
from contextlib import ExitStack

import concourse.bass as bass
from concourse import mybir

ALU = mybir.AluOpType
ACT = mybir.ActivationFunctionType
AX = mybir.AxisListType
F32 = mybir.dt.float32
U32 = mybir.dt.uint32
I32 = mybir.dt.int32

P = 128
SEQ, D = 512, 1024
DEPTH = 2
NT = SEQ // P
KD = D // P
EPS = 1e-6
HD = 64
NH = 4
GROUP_W = NH * HD
ZW = 3 * 512 + 256 + 128 + 32
GRP = 512
Z_CQ, Z_CKV, Z_KR = 1536, 1792, 1920
QKH = 6
MQ = 96
ZCH, ZC = 4, ZW // 4
NEG = -1e30
LOWEST = -3.0e38

PH, PK, TOPK = 8, 128, 16
NEXP = PK * PK
HC = 2 * PH
SLOTS = PH * TOPK
R = 8
HALF = R // 2
UH = SLOTS // HALF
USES = 2 * SLOTS // R
PE_PER_HALF = 3
NDIAG = 6
PE_SLOTS = SLOTS * PE_PER_HALF // HALF
WQ_SLOTS = 12
NQ0 = 4
QB = HC // NQ0
ROUTES = NT + 2

HEADS = [(g, h) for g in (1, 3, 0, 2) for h in range(NH)]
UNITS = len(HEADS) * NT
AHEAD = 3
BANKS = 3


def psum_jobs():
    jobs = []

    def two(kind, n, start=0):
        for i in range(n):
            jobs.append(((kind, i), "ACT" if (i + start) % 2 == 0 else "DVE"))

    two("hT", KD)
    two("z", ZCH * NT)
    two("cT", 3, 1)
    two("qu", NT)
    two("kv", NT)

    def qk(i):
        g, h = HEADS[i]
        jobs.append((("qT", i), "ACT"))
        if g == 3 or h % 2 == 0:
            jobs.append((("kT", i), "DVE"))

    qk(0)
    for u in range(UNITS):
        if u % NT == 0 and u // NT + 1 < len(HEADS):
            qk(u // NT + 1)
        jobs.append((("pT", u), "ACT" if u % 2 else "DVE"))
    two("yT", KD)
    for i in range(2 * NT):
        jobs.append((("out", i), "DVE"))
    two("hT2", KD)
    for i in range(NQ0):
        jobs.append((("q0", i), "ACT"))
    for i in range(HC):
        jobs.append((("qry", i), "ACT"))
    return jobs


JOBS = psum_jobs()
NJ = len(JOBS)
ENG = {name: e for name, e in JOBS}
INDEX = {name: i for i, (name, _) in enumerate(JOBS)}
ORD = {}
COUNT = {"ACT": 0, "DVE": 0}
for _name, _e in JOBS:
    ORD[_name] = COUNT[_e]
    COUNT[_e] += 1


def trunk(nc, x, w_in, w_out, w_q, w_uq, w_ukv, subk, peer_u, peer_v, g_mix, g_ffn, g_group, g_final, g_c, g_qk,
          sink, rope, rope_m, masks, out):
    with ExitStack() as ctx:
        def sb(name, shape, dt=F32):
            return ctx.enter_context(nc.sbuf_tensor(name, shape, dt))

        def sem(name):
            return ctx.enter_context(nc.semaphore(name))

        X = sb("X", [P, NT, D])
        H = sb("H", [P, NT, D])
        HT = sb("HT", [P, KD, SEQ])
        WB = sb("WB", [P, WQ_SLOTS * D])
        QRY = sb("QRY", [P, HC, SEQ])
        SH = sb("SH", [P, NT * ZW + 3 * NT * SEQ])
        GA = sb("GA", [P, D])
        GG = sb("GG", [P, D])
        GC = sb("GC", [P, 384])
        GQK = sb("GQK", [P, 2, HD])
        SK = sb("SK", [P, NH])
        ROPE = sb("ROPE", [P, 4, NT, HD])
        ROPM = sb("ROPM", [P, 2, NT, 32])
        ID = sb("ID", [P, P])
        IOTI = sb("IOTI", [P, TOPK], I32)
        IOT = sb("IOT", [P, TOPK])
        LOFF = sb("LOFF", [P, 1])
        TICK = sb("TICK", [P, 1])
        SS = sb("SS", [P, 32])
        RST = sb("RST", [P, 32])
        MX = sb("MX", [P, 2, NT])
        NM = sb("NM", [P, 2, NT])
        RS = sb("RS", [P, 2, NT])
        RI = sb("RI", [P, 2, NT])
        SE = sb("SE", [P, 2, NT])
        QT = sb("QT", [P, 2, SEQ])
        KT = sb("KT", [P, 2, SEQ])
        BK = ctx.enter_context(nc.psum_tensor("BK", [P, 8, 512], F32))

        hflat = H[:].rearrange("p t d -> p (t d)")
        QU_AT, KC_AT = 0, NT * NH * MQ
        QU = hflat[:, 0:NT * NH * MQ].rearrange("p (t n) -> p t n", t=NT)
        KC = hflat[:, NT * NH * MQ:2 * NT * NH * MQ].rearrange("p (t h n) -> p t h n", t=NT, h=NH)
        VD = hflat[:, 2 * NT * NH * MQ:2 * NT * NH * MQ + NT * GROUP_W].rearrange("p (t n) -> p t n", t=NT)
        scr = HT[:].rearrange("p k s -> p (k s)")
        SCR_D = scr[:, 0:NT * 384].rearrange("p (t n) -> p t n", t=NT)
        SCR_P = scr[:, 2048:2048 + NT * 384].rearrange("p (t n) -> p t n", t=NT)
        SQ = scr[:, 0:NT * NT * GROUP_W].rearrange("p (t g n) -> p t g n", t=NT, g=4)
        qflat = QRY[:].rearrange("p a s -> p (a s)")
        MASK = [qflat[:, i * 2048:(i + 1) * 2048].rearrange("p (t s) -> p t s", t=NT) for i in range(2)]
        WUQ = qflat[:, 4096:4096 + 768].rearrange("p (k n) -> p k n", k=2)
        WUKV = qflat[:, 4864:4864 + 512]
        KTM = qflat[0:MQ, 5376:6400].rearrange("p (b s) -> p b s", b=2)
        Z = SH[:, 0:NT * ZW].rearrange("p (t n) -> p t n", t=NT)
        PR = SH[:, NT * ZW:NT * ZW + 2048].rearrange("p (t s) -> p t s", t=NT)
        PT = SH[:, NT * ZW + 2048:NT * ZW + 3584].rearrange("p (b s) -> p b s", b=3)
        CT = SH[:, NT * ZW + 3584:NT * ZW + 5120].rearrange("p (b s) -> p b s", b=3)
        place = [0]

        def shared(n):
            place[0] += n
            return SH[:, place[0] - n:place[0]]

        SUBK = shared(2048).rearrange("p (a n) -> p a n", a=HC)
        QST = shared(2048).rearrange("p (a n) -> p a n", a=HC)
        HCUR = shared(D)
        ACC = shared(D)
        DIAG = shared(NDIAG * P).rearrange("p (n m) -> p n m", n=NDIAG)
        S12 = shared(HC * TOPK).rearrange("p (a k) -> p a k", a=HC)
        I12 = shared(HC * TOPK).bitcast(U32).rearrange("p (a k) -> p a k", a=HC)
        I12F = shared(HC * TOPK).rearrange("p (a k) -> p a k", a=HC)
        work = [shared(HC * PK), shared(HC * PK)]
        REST = work[0].rearrange("p (a n) -> p a n", a=HC)
        SUMS = work[1].rearrange("p (h n) -> p h n", h=PH)
        ONE = [w.rearrange("p (h k a) -> p h k a", h=PH, k=TOPK) for w in work]
        BEST = shared(SLOTS).rearrange("p (h k) -> p h k", h=PH)
        POS = shared(SLOTS).bitcast(U32).rearrange("p (h k) -> p h k", h=PH)
        PAB = shared(2 * SLOTS).bitcast(U32).rearrange("p (c h k) -> p c h k", c=2, h=PH)
        PABF = shared(2 * SLOTS).rearrange("p (c h k) -> p c h k", c=2, h=PH)
        ISEL = shared(2 * SLOTS).rearrange("p (c h k) -> p c h k", c=2, h=PH)
        EIDX = shared(SLOTS)
        IDXU, IDXV = shared(SLOTS).bitcast(I32), shared(SLOTS).bitcast(I32)
        GE = shared(SLOTS).rearrange("p (h k) -> p h k", h=PH)
        GATE = shared(SLOTS).rearrange("p (h k) -> p h k", h=PH)
        GSUM = shared(PH)
        ADOT = shared(SLOTS)
        AGELU = shared(SLOTS)
        WGT = shared(SLOTS)
        assert place[0] <= NT * ZW + 3 * NT * SEQ

        WZ_AT = [R * D, 0, KD * ZC, R * D]
        WZ = [WB[:, a:a + KD * ZC].rearrange("p (k n) -> p k n", k=KD) for a in WZ_AT]
        WO = WB[:, 0:KD * D].rearrange("p (k n) -> p k n", k=KD)
        WQ = [WB[:, i * D:(i + 1) * D].rearrange("p (k n) -> p k n", k=KD) for i in range(WQ_SLOTS)]
        RING = [WB[:, i * D:(i + 1) * D] for i in range(R)]
        OUT = BK[:, 7, :].rearrange("p (t n) -> p t n", t=NT)
        SC = BK[:, 0:4, :].rearrange("p b (a n) -> p (b a) n", n=PK)
        YV = BK[:, 4:6, :].rearrange("p b n -> p (b n)")

        ld_x, ld_const = sem("ld_x"), sem("ld_const")
        ld_ga, ld_attn, ld_wo, ld_sub, ld_gf = sem("ld_ga"), sem("ld_attn"), sem("ld_wo"), sem("ld_sub"), sem("ld_gf")
        ld_wz = [sem(f"ld_wz{i}") for i in range(ZCH)]
        ld_wq = [sem(f"ld_wq{i}") for i in range(HC)]
        stored = sem("stored")
        ident_done, iota_done = sem("ident_done"), sem("iota_done")
        layer_open = sem("layer_open")
        psum_full = sem("psum_full")
        act_free, dve_free = sem("act_free"), sem("dve_free")
        act_sq, dve_var, act_rt = sem("act_sq"), sem("dve_var"), sem("act_rt")
        h_ready, c_ready = sem("h_ready"), sem("c_ready")
        qkd_ready, b_ready, ac_ready = sem("qkd_ready"), sem("b_ready"), sem("ac_ready")
        s_full, s_max, p_ready, y_ready = sem("s_full"), sem("s_max"), sem("p_ready"), sem("y_ready")
        o_full, o_free = sem("o_full"), sem("o_free")
        q_staged, h_staged, sc_full, sc_used = sem("q_staged"), sem("h_staged"), sem("sc_full"), sem("sc_used")
        best_ready, ge_ready = sem("best_ready"), sem("ge_ready")
        idxu_ready, idxv_ready = sem("idxu_ready"), sem("idxv_ready")
        slot = [sem(f"slot{i}") for i in range(R)]
        used_dve, used_pe = sem("used_dve"), sem("used_pe")
        u_done, gelu_done, w_ready = sem("u_done"), sem("gelu_done"), sem("w_ready")
        diag_ready, v_done, v_taken = sem("diag_ready"), sem("v_done"), sem("v_taken")

        table_u = peer_u.rearrange("l n d -> (l n) d")
        table_v = peer_v.rearrange("l n d -> (l n) d")

        def bank(name):
            return 4 + INDEX[name] % BANKS

        def freed(eng, l, name):
            s = act_free if ENG[name] == "ACT" else dve_free
            eng.wait_ge(s, l * COUNT[ENG[name]] + ORD[name] + 1)

        def full(eng, l, name):
            eng.wait_ge(psum_full, l * NJ + INDEX[name] + 1)

        block = ctx.enter_context(nc.Block())

        @block.sync
        def _(sp):
            sp.dma_start(X[:], x[0].rearrange("(t p) d -> p t d", p=P)).then_inc(ld_x, 16)
            for i in range(4):
                sp.dma_start(ROPE[:, i], rope[i].rearrange("(t p) n -> p t n", p=P)).then_inc(ld_const, 16)
            for i in range(2):
                sp.dma_start(ROPM[:, i], rope_m[i].rearrange("(t p) n -> p t n", p=P)).then_inc(ld_const, 16)
            sp.dma_start(GA[:], g_mix[0:1].broadcast_to([P, D])).then_inc(ld_ga, 16)
            sp.dma_start(WB[:, WZ_AT[0]:WZ_AT[0] + KD * ZC], w_in[0, 0]).then_inc(ld_wz[0], 16)
            with sp.Fori(0, DEPTH) as l:
                sp.wait_ge(layer_open, l + 1)
                for c in (1, 2):
                    sp.dma_start(WB[:, WZ_AT[c]:WZ_AT[c] + KD * ZC], w_in[l, c]).then_inc(ld_wz[c], 16)
                sp.dma_start(GG[:], g_group[bass.ds(l, 1)].broadcast_to([P, D])).then_inc(ld_attn, 16)
                sp.dma_start(GC[:], g_c[bass.ds(l, 1)].broadcast_to([P, 384])).then_inc(ld_attn, 16)
                sp.dma_start(GQK[:].rearrange("p a n -> p (a n)"),
                             g_qk[bass.ds(l, 1)].broadcast_to([P, 2 * HD])).then_inc(ld_attn, 16)
                sp.dma_start(SK[:], sink[bass.ds(l, 1)].broadcast_to([P, NH])).then_inc(ld_attn, 16)
                for i in range(2):
                    sp.dma_start(MASK[i], masks[i].rearrange("(t p) s -> p t s", p=P)).then_inc(ld_attn, 16)
                sp.dma_start(qflat[:, 4096:4096 + 768], w_uq[l]).then_inc(ld_attn, 16)
                sp.dma_start(WUKV, w_ukv[l]).then_inc(ld_attn, 16)
                full(sp, l, ("z", NT - 1))
                sp.dma_start(WB[:, WZ_AT[3]:WZ_AT[3] + KD * ZC], w_in[l, 3]).then_inc(ld_wz[3], 16)
                full(sp, l, ("z", ZCH * NT - 1))
                sp.dma_start(WB[:, 0:KD * D], w_out[l]).then_inc(ld_wo, 16)
                sp.wait_ge(h_ready, l * 2 * NT + NT)
                sp.dma_start(GA[:], g_ffn[bass.ds(l, 1)].broadcast_to([P, D])).then_inc(ld_ga, 16)
                for i in range(HC):
                    s = (i + 8) % WQ_SLOTS
                    if i == 4:
                        full(sp, l, ("out", 2 * NT - 1))
                        sp.dma_start(SH[:, 0:HC * PK], subk[l]).then_inc(ld_sub, 16)
                    if i == WQ_SLOTS:
                        full(sp, l, ("q0", 0))
                    sp.dma_start(WB[:, s * D:(s + 1) * D], w_q[l, i]).then_inc(ld_wq[i], 16)
                nxt = sp.snap((l + 1) % DEPTH)
                sp.wait_ge(h_ready, (l + 1) * 2 * NT)
                sp.dma_start(GA[:], g_mix[bass.ds(nxt, 1)].broadcast_to([P, D])).then_inc(ld_ga, 16)
                for i in range(HC - QB):
                    full(sp, l, ("qry", i))
                    s = R + i % QB
                    sp.dma_start(WB[:, s * D:(s + 1) * D], w_q[l, i]).then_inc(ld_wq[i], 16)
                full(sp, l, ("qry", HC - 1))
                sp.dma_start(WB[:, WZ_AT[0]:WZ_AT[0] + KD * ZC], w_in[nxt, 0]).then_inc(ld_wz[0], 16)
            sp.wait_ge(layer_open, DEPTH + 1)
            sp.wait_ge(ld_ga, DEPTH * 32 + 16)
            sp.wait_ge(ld_wz[0], (DEPTH + 1) * 16)
            sp.dma_start(GA[:], g_final.broadcast_to([P, D])).then_inc(ld_gf, 16)
            for t in range(NT):
                sp.wait_ge(h_ready, DEPTH * 2 * NT + t + 1)
                sp.dma_start(out[0, t * P:(t + 1) * P, :], H[:, t, :]).then_inc(stored, 16)
            sp.wait_ge(stored, 16 * NT)

        @block.gpsimd
        def _(pool):
            dve_need, pe_need = pool.alloc_register("dve_need"), pool.alloc_register("pe_need")
            u_need, v_need = pool.alloc_register("u_need"), pool.alloc_register("v_need")
            nc.gpsimd.memset(ID[:], 0.0)
            pool.drain()
            nc.gpsimd.affine_select(out=ID[:], in_=ID[:], compare_op=ALU.not_equal, fill=1.0, base=0,
                                    pattern=[[-1, P]], channel_multiplier=1).then_inc(ident_done, 1)
            nc.gpsimd.iota(IOTI[:], [[1, TOPK]], base=0, channel_multiplier=0).then_inc(iota_done, 1)
            pool.wait_ge(ld_const, 16 * 6)
            pool.reg_mov(dve_need, 1)
            pool.reg_mov(pe_need, PE_PER_HALF)
            pool.reg_mov(u_need, 1)
            pool.reg_mov(v_need, 1)
            with pool.Fori(0, DEPTH) as l:
                freed(pool, l, ("z", ZCH * NT - 2))
                freed(pool, l, ("z", ZCH * NT - 1))
                for g in (0, 2):
                    zz = Z[:, :, g * GRP:g * GRP + QKH * HD].rearrange("p t (h n) -> p t h n", n=HD)
                    sc = SCR_P.rearrange("p t (h n) -> p t h n", n=HD)
                    cos = ROPE[:, 0].unsqueeze(2).broadcast_to([P, NT, QKH, HD])
                    sin = ROPE[:, 1].unsqueeze(2).broadcast_to([P, NT, QKH, HD])
                    nc.gpsimd.tensor_tensor(sc[:, :, :, 0:32], zz[:, :, :, 32:64], sin[:, :, :, 0:32], ALU.mult)
                    nc.gpsimd.tensor_tensor(sc[:, :, :, 32:64], zz[:, :, :, 0:32], sin[:, :, :, 32:64], ALU.mult)
                    pool.drain()
                    nc.gpsimd.tensor_tensor(zz, zz, cos, ALU.mult)
                    pool.drain()
                    nc.gpsimd.tensor_tensor(zz, zz, sc, ALU.add).then_inc(ac_ready, 1)
                    pool.drain()

                def ring_free(k):
                    v_before = k < 2 or k >= UH + 2
                    pool.wait_ge(used_dve, dve_need)
                    pool.reg_add(dve_need, dve_need, HALF if 1 <= k <= UH else 1)
                    if v_before:
                        pool.wait_ge(used_pe, pe_need)
                        pool.reg_add(pe_need, pe_need, PE_PER_HALF)

                def gather(table, idx, s):
                    nc.gpsimd.indirect_dma_start(
                        out=RING[s % R], out_offset=None, in_=table,
                        in_offset=bass.IndirectOffsetOnAxis(ap=idx[:, s:s + 1], axis=0)).then_inc(slot[s % R], 16)

                with pool.Fori(0, NT) as t:
                    pool.wait_ge(idxu_ready, u_need)
                    pool.reg_add(u_need, u_need, 1)
                    for s in range(SLOTS):
                        if s == SLOTS // 2:
                            pool.wait_ge(idxu_ready, u_need)
                            pool.reg_add(u_need, u_need, 1)
                        if s % HALF == 0:
                            ring_free(s // HALF)
                        gather(table_u, IDXU, s)
                    pool.wait_ge(idxv_ready, v_need)
                    pool.reg_add(v_need, v_need, 1)
                    for s in range(SLOTS):
                        if s % HALF == 0:
                            ring_free(UH + s // HALF)
                        gather(table_v, IDXV, s)
                pool.reg_add(u_need, u_need, 2)

        @block.tensor
        def _(pe):
            pe.wait_ge(ident_done, 1)
            pe.wait_ge(ld_const, 16 * 6)
            with pe.Fori(0, DEPTH) as l:
                def begin(name):
                    i = INDEX[name]
                    if i >= BANKS:
                        freed(pe, l, JOBS[i - BANKS][0])
                    return BK[:, bank(name), :]

                def transpose_tokens(kind, src, ready):
                    for k in range(KD):
                        b = begin((kind, k))
                        for t in range(NT):
                            if k == 0:
                                ready(t)
                            ins = nc.tensor.transpose(b[:, t * P:(t + 1) * P], src(t, k), ID[:])
                        ins.then_inc(psum_full, 1)

                def transposed(kind):
                    freed(pe, l, (kind, KD - 2))
                    freed(pe, l, (kind, KD - 1))

                transpose_tokens("hT", lambda t, k: H[:, t, k * P:(k + 1) * P],
                                 lambda t: pe.wait_ge(h_ready, l * 2 * NT + t + 1))
                transposed("hT")
                for c in range(ZCH):
                    pe.wait_ge(ld_wz[c], (l + 1) * 16)
                    for t in range(NT):
                        name = ("z", c * NT + t)
                        b = begin(name)
                        for k in range(KD):
                            ins = nc.tensor.matmul(b[:, 0:ZC], HT[:, k, t * P:(t + 1) * P], WZ[c][:, k, :],
                                                   start=(k == 0), stop=(k == KD - 1))
                        ins.then_inc(psum_full, 1)
                pe.wait_ge(c_ready, l + 1)
                pe.wait_ge(ld_attn, (l + 1) * 16 * 8)
                for k in range(3):
                    b = begin(("cT", k))
                    for t in range(NT):
                        ins = nc.tensor.transpose(b[:, t * P:(t + 1) * P],
                                                  Z[:, t, Z_CQ + k * P:Z_CQ + (k + 1) * P], ID[:])
                    ins.then_inc(psum_full, 1)
                freed(pe, l, ("cT", 1))
                freed(pe, l, ("cT", 2))
                for t in range(NT):
                    b = begin(("qu", t))
                    for k in range(2):
                        ins = nc.tensor.matmul(b[:, 0:NH * MQ], CT[:, k, t * P:(t + 1) * P], WUQ[:, k, :],
                                               start=(k == 0), stop=(k == 1))
                    ins.then_inc(psum_full, 1)
                for t in range(NT):
                    b = begin(("kv", t))
                    nc.tensor.matmul(b, CT[:, 2, t * P:(t + 1) * P], WUKV, start=True, stop=True).then_inc(psum_full, 1)

                def queries(i):
                    g, h = HEADS[i]
                    if h == 0:
                        if g == 1:
                            pe.wait_ge(b_ready, l + 1)
                        elif g == 3:
                            pe.wait_ge(qkd_ready, l + 1)
                        else:
                            pe.wait_ge(ac_ready, l * 2 + (1 if g == 0 else 2))
                    b = begin(("qT", i))
                    for t in range(NT):
                        q = QU_AT + (t * NH + h) * MQ
                        src = hflat[:, q:q + P] if g == 3 else Z[:, t, g * GRP + h * HD:g * GRP + h * HD + P]
                        ins = nc.tensor.transpose(b[:, t * P:(t + 1) * P], src, ID[:])
                    ins.then_inc(psum_full, 1)
                    if ("kT", i) in INDEX:
                        b = begin(("kT", i))
                        for t in range(NT):
                            c = g * GRP + GROUP_W + h // 2 * HD
                            k = KC_AT + (t * NH + h) * MQ
                            src = hflat[:, k:k + P] if g == 3 else Z[:, t, c:c + P]
                            ins = nc.tensor.transpose(b[:, t * P:(t + 1) * P], src, ID[:])
                        ins.then_inc(psum_full, 1)

                def scores(u):
                    i, t = u // NT, u % NT
                    g, h = HEADS[i]
                    w = MQ if g == 3 else P
                    keys = KTM[:, h % 2, :] if g == 3 else KT[:, (h // 2) % 2, :]
                    if t == 0:
                        freed(pe, l, ("qT", i))
                        if ("kT", i) in INDEX:
                            freed(pe, l, ("kT", i))
                    if u >= NT:
                        if HEADS[(u - NT) // NT][0] in (0, 2):
                            pe.wait_ge(s_max, l * UNITS + u - NT + 1)
                        else:
                            pe.wait_ge(p_ready, l * UNITS + u - NT + 1)
                    nc.tensor.matmul(BK[:, t, :], QT[0:w, i % 2, t * P:(t + 1) * P], keys, start=True, stop=True)\
                        .then_inc(s_full, 1)

                def turn(u):
                    pe.wait_ge(p_ready, l * UNITS + u + 1)
                    b = begin(("pT", u))
                    for kt in range(NT):
                        ins = nc.tensor.transpose(b[:, kt * P:(kt + 1) * P], PR[:, u % NT, kt * P:(kt + 1) * P], ID[:])
                    ins.then_inc(psum_full, 1)

                def product(u):
                    i, t = u // NT, u % NT
                    g, h = HEADS[i]
                    freed(pe, l, ("pT", u))
                    if t == 0:
                        pe.wait_ge(o_free, l * len(HEADS) + i + 1)
                    for kt in range(NT):
                        c = g * GRP + GROUP_W + 2 * HD
                        v = VD[:, kt, h // 2 * P:h // 2 * P + P] if g == 3 else Z[:, kt, c:c + P]
                        ins = nc.tensor.matmul(OUT[:, t, :], PT[:, u % 3, kt * P:(kt + 1) * P], v,
                                               start=(kt == 0), stop=(kt == NT - 1))
                    ins.then_inc(o_full, 1)

                queries(0)
                for u in range(AHEAD):
                    scores(u)
                for u in range(UNITS):
                    if u % NT == 0 and u // NT + 1 < len(HEADS):
                        queries(u // NT + 1)
                    if u + AHEAD < UNITS:
                        scores(u + AHEAD)
                    turn(u)
                    if u > 0:
                        product(u - 1)
                product(UNITS - 1)

                transpose_tokens("yT", lambda t, k: Z[:, t, k // 2 * GRP + k % 2 * P:k // 2 * GRP + k % 2 * P + P],
                                 lambda t: pe.wait_ge(y_ready, l + 1) if t == 0 else None)
                transposed("yT")
                pe.wait_ge(ld_wo, (l + 1) * 16)
                for t in range(NT):
                    for n in range(2):
                        b = begin(("out", 2 * t + n))
                        for k in range(KD):
                            ins = nc.tensor.matmul(b, HT[:, k, t * P:(t + 1) * P], WO[:, k, n * 512:(n + 1) * 512],
                                                   start=(k == 0), stop=(k == KD - 1))
                        ins.then_inc(psum_full, 1)

                transpose_tokens("hT2", lambda t, k: H[:, t, k * P:(k + 1) * P],
                                 lambda t: pe.wait_ge(h_ready, l * 2 * NT + NT + t + 1))
                transposed("hT2")

                def key_scores(lists):
                    for a in lists:
                        ins = nc.tensor.matmul(SC[:, a, :], QST[:, a, :], SUBK[:, a, :], start=True, stop=True)
                    ins.then_inc(sc_full, 1)

                for i in range(NQ0):
                    b = begin(("q0", i))
                    for m in range(QB):
                        a = i * QB + m
                        pe.wait_ge(ld_wq[a], l * (32 if a < HC - QB else 16) + 16)
                        for k in range(KD):
                            ins = nc.tensor.matmul(b[:, m * P:(m + 1) * P], WQ[(a + 8) % WQ_SLOTS][:, k, :],
                                                   HT[:, k, 0:P], start=(k == 0), stop=(k == KD - 1))
                    ins.then_inc(psum_full, 1)
                    if i == 2:
                        pe.wait_ge(ld_sub, (l + 1) * 16)
                        freed(pe, l, ("q0", 1))
                        key_scores(range(HC // 2))
                freed(pe, l, ("q0", 3))
                key_scores(range(HC // 2, HC))
                for i in range(HC):
                    a = (i + HC - QB) % HC
                    b = begin(("qry", i))
                    if i >= QB:
                        pe.wait_ge(ld_wq[a], (l + 1) * 32)
                    for k in range(KD):
                        ins = nc.tensor.matmul(b[:, 0:SEQ - P], WQ[R + i % QB][:, k, :], HT[:, k, P:SEQ],
                                               start=(k == 0), stop=(k == KD - 1))
                    ins.then_inc(psum_full, 1)
                with pe.Fori(0, NT) as t:
                    T = pe.snap(l * NT + t)
                    pe.wait_ge(sc_used, l * ROUTES + t + 2)
                    pe.wait_ge(q_staged, T + 1)
                    key_scores(range(HC))
                    rows = pe.snap(T * (USES * 16))
                    diags = pe.snap(T * PE_SLOTS)
                    pe.wait_ge(v_taken, T + 1)
                    freed(pe, l, ("qry", HC - 1))
                    n = 0
                    for s in range(SLOTS):
                        if s % HALF == HALF - 1:
                            continue
                        pe.wait_ge(diag_ready, diags + (n + 1))
                        pe.wait_ge(slot[s % R], rows + (SLOTS // R + s // R + 1) * 16)
                        for b in range(2):
                            ins = nc.tensor.matmul(BK[:, 4 + b, :], DIAG[:, n % NDIAG, :],
                                                   RING[s % R][:, b * 512:(b + 1) * 512],
                                                   start=(n == 0), stop=(n == PE_SLOTS - 1))
                        ins.then_inc(used_pe, 1)
                        n += 1

        @block.scalar
        def _(act):
            def copy_out(l, name, dst, src):
                full(act, l, name)
                nc.scalar.copy(dst, src).then_inc(act_free, 1)

            def square_sums(l, n):
                for t in range(NT):
                    nc.scalar.activation(H[:, t, :], X[:, t, :], ACT.Square, accum_out=SS[:, t:t + 1]).then_inc(act_sq, 1)

            def root(l, n, cols):
                act.wait_ge(dve_var, l * 4 + n + 1)
                nc.scalar.activation(RST[:, 0:cols], SS[:, 0:cols], ACT.Sqrt).then_inc(act_rt, 1)

            act.wait_ge(ld_x, 16)
            act.wait_ge(ident_done, 1)
            with act.Fori(0, DEPTH) as l:
                act.wait_ge(layer_open, l + 1)
                square_sums(l, 0)
                root(l, 0, NT)
                for k in range(0, KD, 2):
                    copy_out(l, ("hT", k), HT[:, k, :], BK[:, bank(("hT", k)), :])
                for i in range(0, ZCH * NT, 2):
                    c, t = i // NT, i % NT
                    copy_out(l, ("z", i), Z[:, t, c * ZC:(c + 1) * ZC], BK[:, bank(("z", i)), 0:ZC])
                root(l, 1, 32)
                copy_out(l, ("cT", 1), CT[:, 1, :], BK[:, bank(("cT", 1)), :])
                for t in range(0, NT, 2):
                    copy_out(l, ("qu", t), QU[:, t, :], BK[:, bank(("qu", t)), 0:NH * MQ])
                for t in range(0, NT, 2):
                    kv = BK[:, bank(("kv", t)), :].rearrange("p (h n) -> p h n", h=NH)
                    full(act, l, ("kv", t))
                    nc.scalar.copy(KC[:, t, :, 0:HD], kv[:, :, 0:HD])
                    nc.scalar.copy(VD[:, t, :].rearrange("p (h n) -> p h n", h=NH), kv[:, :, HD:2 * HD]).then_inc(act_free, 1)

                def queries(i):
                    w = MQ if HEADS[i][0] == 3 else P
                    copy_out(l, ("qT", i), QT[0:w, i % 2, :], BK[0:w, bank(("qT", i)), :])

                def probs(u):
                    i, t = u // NT, u % NT
                    g, h = HEADS[i]
                    act.wait_ge(s_max, l * UNITS + u + 1)
                    if u >= NT:
                        full(act, l, ("pT", u - NT))
                    bias = NM[:, i % 2, t:t + 1]
                    rows = RS[:, i % 2, t:t + 1]
                    if g in (0, 2):
                        ins = nc.scalar.activation(PR[:, t, :], PR[:, t, :], ACT.Exp, bias=bias, accum_out=rows)
                    else:
                        ins = nc.scalar.activation(PR[:, t, :], BK[:, t, :], ACT.Exp, bias=bias,
                                                   scale=(MQ if g == 3 else HD) ** -0.5, accum_out=rows)
                    if g == 0 and t == NT - 1:
                        ins = nc.scalar.activation(SE[:, i % 2, :], NM[:, i % 2, :], ACT.Exp, bias=SK[:, h:h + 1])
                    ins.then_inc(p_ready, 1)

                act.wait_ge(ld_attn, (l + 1) * 16 * 8)
                queries(0)
                for u in range(AHEAD - 1):
                    probs(u)
                for u in range(UNITS):
                    if u % NT == 0 and u // NT + 1 < len(HEADS):
                        queries(u // NT + 1)
                    if u + AHEAD - 1 < UNITS:
                        probs(u + AHEAD - 1)
                    if u % 2:
                        if u >= 3:
                            act.wait_ge(o_full, l * UNITS + u - 2)
                        copy_out(l, ("pT", u), PT[:, u % 3, :], BK[:, bank(("pT", u)), :])
                act.wait_ge(o_free, (l + 1) * len(HEADS) + 1)
                for g in range(4):
                    ins = nc.scalar.activation(SQ[:, :, g, :], Z[:, :, g * GRP:g * GRP + GROUP_W], ACT.Square)
                ins.then_inc(act_sq, 1)
                root(l, 2, 16)
                for k in range(0, KD, 2):
                    copy_out(l, ("yT", k), HT[:, k, :], BK[:, bank(("yT", k)), :])
                freed(act, l, ("out", 2 * NT - 1))
                square_sums(l, 1)
                root(l, 3, NT)
                for k in range(0, KD, 2):
                    copy_out(l, ("hT2", k), HT[:, k, :], BK[:, bank(("hT2", k)), :])
                for i in range(NQ0):
                    copy_out(l, ("q0", i), QST[:, i * QB:(i + 1) * QB, :].rearrange("p a n -> p (a n)"),
                             BK[:, bank(("q0", i)), :])

                def queries_out(n):
                    for i in n:
                        copy_out(l, ("qry", i), QRY[:, (i + HC - QB) % HC, P:SEQ],
                                 BK[:, bank(("qry", i)), 0:SEQ - P])

                act.wait_ge(h_ready, (l + 1) * 2 * NT)
                nc.scalar.copy(HCUR, H[:, 0, :]).then_inc(h_staged, 1)
                queries_out(range(HC // 2))
                act.wait_ge(best_ready, l * (NT + 1) + 1)
                nc.scalar.activation(GE, GE, ACT.Exp).then_inc(ge_ready, 1)
                queries_out(range(HC // 2, HC))
                act.drain()
                with act.Fori(0, NT) as t:
                    T = act.snap(l * NT + t)
                    nxt = act.snap(t % (NT - 1) + 1)
                    act.wait_ge(sc_full, l * ROUTES + t + 2)
                    nc.scalar.copy(QST, QRY[:, :, bass.ds(nxt * P, P)]).then_inc(q_staged, 1)
                    act.wait_ge(u_done, T + 1)
                    nc.scalar.activation(AGELU, ADOT, ACT.Gelu).then_inc(gelu_done, 1)
                    nc.scalar.copy(HCUR, H[:, bass.ds(nxt, 1), :].rearrange("p a d -> p (a d)")).then_inc(h_staged, 1)
                    used = act.snap(T * PE_SLOTS + PE_PER_HALF * 2)
                    act.wait_ge(w_ready, T + 1)
                    n = 0
                    for s in range(SLOTS):
                        if s % HALF == HALF - 1:
                            continue
                        if n % PE_PER_HALF == 0:
                            act.wait_ge(used_pe, used + (n - NDIAG + PE_PER_HALF))
                        nc.scalar.activation(DIAG[:, n % NDIAG, :], ID[:], ACT.Copy,
                                             scale=WGT[:, s:s + 1]).then_inc(diag_ready, 1)
                        n += 1
                    act.wait_ge(best_ready, l * (NT + 1) + t + 2)
                    nc.scalar.activation(GE, GE, ACT.Exp).then_inc(ge_ready, 1)
            act.wait_ge(layer_open, DEPTH + 1)
            square_sums(DEPTH, 0)
            act.wait_ge(dve_var, DEPTH * 4 + 1)
            nc.scalar.activation(RST[:, 0:NT], SS[:, 0:NT], ACT.Sqrt).then_inc(act_rt, 1)

        @block.vector
        def _(dve):
            v = nc.vector

            def arrived():
                v.tensor_copy(TICK[:], LOFF[:])
                dve.drain()

            def copy_out(l, name, dst, src):
                full(dve, l, name)
                v.tensor_copy(dst, src).then_inc(dve_free, 1)

            def rstd(l, n, widths):
                at = 0
                for cols, width in widths:
                    ins = v.tensor_scalar(SS[:, at:at + cols], SS[:, at:at + cols], 1.0 / width, EPS, ALU.mult, ALU.add)
                    at += cols
                ins.then_inc(dve_var, 1)
                dve.wait_ge(act_rt, l * 4 + n + 1)
                v.reciprocal(RST[:, 0:at], RST[:, 0:at])
                dve.drain()

            def normalise(l, n, squares):
                dve.wait_ge(act_sq, l * (2 * NT + 1) + squares + NT)
                rstd(l, n, [(NT, D)])
                for t in range(NT):
                    v.scalar_tensor_tensor(H[:, t, :], X[:, t, :], RST[:, t:t + 1], GA[:], ALU.mult, ALU.mult)\
                        .then_inc(h_ready, 1)

            v.memset(LOFF[:], 0.0)
            v.memset(KT[:], 0.0)
            v.memset(MX[:], 0.0).then_inc(used_dve, 2)
            v.memset(NM[:], 0.0).then_inc(used_pe, 2 * PE_PER_HALF)
            v.memset(RI[:], 0.0).then_inc(v_taken, 1)
            v.memset(RS[:], 0.0).then_inc(o_free, 1)
            v.memset(SS[:], 0.0).then_inc(layer_open, 1)
            dve.wait_ge(iota_done, 1)
            v.tensor_copy(IOT[:], IOTI[:])
            dve.wait_ge(ld_x, 16)
            dve.wait_ge(ld_const, 16 * 6)
            dve.drain()
            with dve.Fori(0, DEPTH) as l:
                dve.wait_ge(ld_ga, l * 32 + 16)
                normalise(l, 0, 0)
                for k in range(1, KD, 2):
                    copy_out(l, ("hT", k), HT[:, k, :], BK[:, bank(("hT", k)), :])
                for i in range(1, ZCH * NT, 2):
                    c, t = i // NT, i % NT
                    copy_out(l, ("z", i), Z[:, t, c * ZC:(c + 1) * ZC], BK[:, bank(("z", i)), 0:ZC])
                dve.drain()
                dve.wait_ge(ld_attn, (l + 1) * 16 * 8)
                freed(dve, l, ("z", ZCH * NT - 2))

                zb = Z[:, :, GRP:GRP + QKH * HD]
                zbh = zb.rearrange("p t (h n) -> p t h n", n=HD)
                zc = Z[:, :, Z_CQ:Z_CQ + 384]
                sh = SCR_D.rearrange("p t (h n) -> p t h n", n=HD)
                v.tensor_tensor(SCR_D, zb, zb, ALU.mult)
                dve.drain()
                v.tensor_reduce(SS[:, 0:24].rearrange("p (t h) -> p t h", t=NT), sh, AX.X, ALU.add)
                dve.drain()
                v.tensor_tensor(SCR_D, zc, zc, ALU.mult)
                dve.drain()
                v.tensor_reduce(SS[:, 24:28], SCR_D[:, :, 0:256], AX.X, ALU.add)
                v.tensor_reduce(SS[:, 28:32], SCR_D[:, :, 256:384], AX.X, ALU.add)
                dve.drain()
                rstd(l, 1, [(24, HD), (4, 256), (4, 128)])
                for t in range(NT):
                    v.scalar_tensor_tensor(Z[:, t, Z_CQ:Z_CQ + 256], Z[:, t, Z_CQ:Z_CQ + 256], RST[:, 24 + t:25 + t],
                                           GC[:, 0:256], ALU.mult, ALU.mult)
                    ins = v.scalar_tensor_tensor(Z[:, t, Z_CKV:Z_CKV + 128], Z[:, t, Z_CKV:Z_CKV + 128],
                                                 RST[:, 28 + t:29 + t], GC[:, 256:384], ALU.mult, ALU.mult)
                ins.then_inc(c_ready, 1)
                rb = RST[:, 0:24].rearrange("p (t h) -> p t h", t=NT).unsqueeze(3).broadcast_to([P, NT, QKH, HD])
                v.tensor_tensor(zbh, zbh, rb, ALU.mult)
                dve.drain()
                for a, (h0, h1) in enumerate(((0, NH), (NH, QKH))):
                    gain = GQK[:, a, :].unsqueeze(1).unsqueeze(1).broadcast_to([P, NT, h1 - h0, HD])
                    v.tensor_tensor(zbh[:, :, h0:h1, :], zbh[:, :, h0:h1, :], gain, ALU.mult)
                dve.drain()
                for r in range(2):
                    for a, b in ((0, 16), (16, 0)):
                        o, i = 32 * r + a, 32 * r + b
                        v.tensor_tensor(sh[:, :, :, o:o + 16], zbh[:, :, :, i:i + 16],
                                        ROPE[:, 3, :, o:o + 16].unsqueeze(2).broadcast_to([P, NT, QKH, 16]), ALU.mult)
                dve.drain()
                v.tensor_tensor(zbh, zbh, ROPE[:, 2].unsqueeze(2).broadcast_to([P, NT, QKH, HD]), ALU.mult)
                dve.drain()
                v.tensor_tensor(zbh, zbh, sh, ALU.add).then_inc(b_ready, 1)
                dve.drain()

                for k in (0, 2):
                    copy_out(l, ("cT", k), CT[:, k, :], BK[:, bank(("cT", k)), :])
                for t in range(1, NT, 2):
                    copy_out(l, ("qu", t), QU[:, t, :], BK[:, bank(("qu", t)), 0:NH * MQ])
                for t in range(1, NT, 2):
                    kv = BK[:, bank(("kv", t)), :].rearrange("p (h n) -> p h n", h=NH)
                    full(dve, l, ("kv", t))
                    v.tensor_copy(KC[:, t, :, 0:HD], kv[:, :, 0:HD])
                    v.tensor_copy(VD[:, t, :].rearrange("p (h n) -> p h n", h=NH), kv[:, :, HD:2 * HD]).then_inc(dve_free, 1)
                dve.drain()
                freed(dve, l, ("kv", NT - 2))
                qr = QU.rearrange("p t (h n) -> p t h n", n=MQ)
                kr = Z[:, :, Z_KR:Z_KR + 32]
                sq = SCR_D[:, :, 0:128].rearrange("p t (h n) -> p t h n", n=32)
                sk = SCR_D[:, :, 128:160]
                for a, b in ((0, 16), (16, 0)):
                    v.tensor_tensor(sq[:, :, :, a:a + 16], qr[:, :, :, 64 + b:80 + b],
                                    ROPM[:, 1, :, a:a + 16].unsqueeze(2).broadcast_to([P, NT, NH, 16]), ALU.mult)
                    v.tensor_tensor(sk[:, :, a:a + 16], kr[:, :, b:b + 16], ROPM[:, 1, :, a:a + 16], ALU.mult)
                dve.drain()
                v.tensor_tensor(qr[:, :, :, 64:96], qr[:, :, :, 64:96],
                                ROPM[:, 0].unsqueeze(2).broadcast_to([P, NT, NH, 32]), ALU.mult)
                v.tensor_tensor(kr, kr, ROPM[:, 0], ALU.mult)
                dve.drain()
                v.tensor_tensor(qr[:, :, :, 64:96], qr[:, :, :, 64:96], sq, ALU.add)
                for h in range(NH):
                    ins = v.tensor_tensor(KC[:, :, h, HD:MQ], kr, sk, ALU.add)
                ins.then_inc(qkd_ready, 1)

                def keys(i):
                    if ("kT", i) in INDEX:
                        g, h = HEADS[i]
                        w = MQ if g == 3 else HD
                        dst = KTM[:, h % 2, :] if g == 3 else KT[0:HD, (h // 2) % 2, :]
                        copy_out(l, ("kT", i), dst, BK[0:w, bank(("kT", i)), :])

                def maxima(u):
                    i, t = u // NT, u % NT
                    g, h = HEADS[i]
                    mx, nm = MX[:, i % 2, t:t + 1], NM[:, i % 2, t:t + 1]
                    if u >= NT:
                        full(dve, l, ("pT", u - NT))
                    dve.wait_ge(s_full, l * UNITS + u + 1)
                    if g in (0, 2):
                        arrived()
                        v.tensor_tensor_reduce(out=PR[:, t, :], in0=BK[:, t, :], in1=MASK[g // 2][:, t, :],
                                               scale=HD ** -0.5, scalar=LOWEST, op0=ALU.add, op1=ALU.max, accum_out=mx)
                    else:
                        v.tensor_reduce(mx, BK[:, t, :], AX.X, ALU.max)
                    dve.drain()
                    if g == 0:
                        v.tensor_scalar(nm, mx, SK[:, h:h + 1], -1.0, ALU.max, ALU.mult).then_inc(s_max, 1)
                    else:
                        scale = -1.0 if g == 2 else -(MQ if g == 3 else HD) ** -0.5
                        v.tensor_scalar(nm, mx, scale, None, ALU.mult).then_inc(s_max, 1)

                def output(i):
                    g, h = HEADS[i]
                    dve.wait_ge(p_ready, l * UNITS + (i + 1) * NT)
                    if g == 0:
                        v.tensor_tensor(RS[:, i % 2, :], RS[:, i % 2, :], SE[:, i % 2, :], ALU.add)
                        dve.drain()
                    v.reciprocal(RI[:, i % 2, :], RS[:, i % 2, :])
                    dve.drain()
                    dve.wait_ge(o_full, l * UNITS + (i + 1) * NT)
                    half = (h % 2 if g == 3 else h // 2) * HD
                    v.tensor_tensor(Z[:, :, g * GRP + h * HD:g * GRP + (h + 1) * HD], OUT[:, :, half:half + HD],
                                    RI[:, i % 2, :].unsqueeze(2).broadcast_to([P, NT, HD]), ALU.mult).then_inc(o_free, 1)

                keys(0)
                for u in range(AHEAD):
                    maxima(u)
                for u in range(UNITS):
                    if u % NT == 0 and u // NT + 1 < len(HEADS):
                        keys(u // NT + 1)
                    if u + AHEAD < UNITS:
                        maxima(u + AHEAD)
                    if u % 2 == 0:
                        if u >= 3:
                            dve.wait_ge(o_full, l * UNITS + u - 2)
                        copy_out(l, ("pT", u), PT[:, u % 3, :], BK[:, bank(("pT", u)), :])
                    if u % NT == 0 and u > 0:
                        output(u // NT - 1)
                output(len(HEADS) - 1)

                dve.wait_ge(act_sq, l * (2 * NT + 1) + NT + 1)
                v.tensor_reduce(SS[:, 0:16].rearrange("p (t g) -> p t g", t=NT), SQ, AX.X, ALU.add)
                dve.drain()
                rstd(l, 2, [(16, GROUP_W)])
                for t in range(NT):
                    for g in range(4):
                        zo = Z[:, t, g * GRP:g * GRP + GROUP_W]
                        ins = v.scalar_tensor_tensor(zo, zo, RST[:, 4 * t + g:4 * t + g + 1],
                                                     GG[:, g * GROUP_W:(g + 1) * GROUP_W], ALU.mult, ALU.mult)
                ins.then_inc(y_ready, 1)
                for k in range(1, KD, 2):
                    copy_out(l, ("yT", k), HT[:, k, :], BK[:, bank(("yT", k)), :])
                for t in range(NT):
                    for n in range(2):
                        name = ("out", 2 * t + n)
                        xs = X[:, t, n * 512:(n + 1) * 512]
                        full(dve, l, name)
                        v.tensor_tensor(xs, xs, BK[:, bank(name), :], ALU.add).then_inc(dve_free, 1)
                dve.wait_ge(ld_ga, (l + 1) * 32)
                normalise(l, 3, NT + 1)
                for k in range(1, KD, 2):
                    copy_out(l, ("hT2", k), HT[:, k, :], BK[:, bank(("hT2", k)), :])

                def route_steps(h0=0, h1=PH):
                    lists, heads, hs = range(2 * h0, 2 * h1), range(h0, h1), slice(h0, h1)
                    halves = (slice(0, 8), slice(8, 16))
                    sums = SUMS.rearrange("p h (a b) -> p h a b", a=TOPK)[:, hs]
                    s12 = S12.rearrange("p (h c) k -> p h c k", c=2)[:, hs]
                    i12 = I12F.rearrange("p (h c) k -> p h c k", c=2)[:, hs]
                    full4 = [P, h1 - h0, TOPK, TOPK]
                    full3 = [P, h1 - h0, TOPK]

                    def list_max():
                        for a in lists:
                            v.max(S12[:, a, 0:8], SC[:, a, :])

                    def list_index():
                        for a in lists:
                            v.max_index(I12[:, a, 0:8], S12[:, a, 0:8], SC[:, a, :])

                    def list_rest():
                        for a in lists:
                            ins = v.match_replace(REST[:, a, :], S12[:, a, 0:8], SC[:, a, :], LOWEST)
                        ins.then_inc(sc_used, 1)

                    def rest_max():
                        for a in lists:
                            v.max(S12[:, a, 8:16], REST[:, a, :])

                    def rest_index():
                        for a in lists:
                            v.max_index(I12[:, a, 8:16], S12[:, a, 8:16], REST[:, a, :])

                    def all_sums():
                        v.tensor_tensor(sums, s12[:, :, 0, :].unsqueeze(3).broadcast_to(full4),
                                        s12[:, :, 1, :].unsqueeze(2).broadcast_to(full4), ALU.add)
                        ls = slice(2 * h0, 2 * h1)
                        v.tensor_copy(I12F[:, ls], I12[:, ls])

                    def sum_max(part):
                        for h in heads:
                            v.max(BEST[:, h, halves[part]], SUMS[:, h, :])

                    def sum_index(part):
                        for h in heads:
                            v.max_index(POS[:, h, halves[part]], BEST[:, h, halves[part]], SUMS[:, h, :])

                    def sum_rest():
                        for h in heads:
                            v.match_replace(SUMS[:, h, :], BEST[:, h, 0:8], SUMS[:, h, :], LOWEST)

                    def places():
                        v.tensor_scalar(PAB[:, 0, hs], POS[:, hs], 4, None, ALU.logical_shift_right)
                        v.tensor_scalar(PAB[:, 1, hs], POS[:, hs], 15, None, ALU.bitwise_and)

                    def places_float():
                        v.tensor_copy(PABF[:, :, hs], PAB[:, :, hs])

                    def match(c):
                        v.tensor_tensor(ONE[c][:, hs], IOT[:].unsqueeze(1).unsqueeze(1).broadcast_to(full4),
                                        PABF[:, c, hs].unsqueeze(3).broadcast_to(full4), ALU.is_equal)

                    def pick(c):
                        v.tensor_tensor(ONE[c][:, hs], ONE[c][:, hs], i12[:, :, c, :].unsqueeze(2).broadcast_to(full4),
                                        ALU.mult)

                    def add_up(c):
                        v.tensor_reduce(ISEL[:, c, hs], ONE[c][:, hs], AX.X, ALU.add)

                    def experts():
                        v.scalar_tensor_tensor(EIDX.rearrange("p (h k) -> p h k", h=PH)[:, hs], ISEL[:, 0, hs],
                                               float(PK), ISEL[:, 1, hs], ALU.mult, ALU.add)

                    def rows_and_best():
                        at = slice(h0 * TOPK, h1 * TOPK)
                        if h1 < PH:
                            full(dve, l, ("q0", NQ0 - 1))
                        v.tensor_scalar(IDXU[:, at], EIDX[:, at], LOFF[:, 0:1], None, ALU.add)\
                            .then_inc(idxu_ready, 2 * (h1 - h0) // PH)
                        ins = v.tensor_tensor(GE[:, hs], BEST[:, hs], BEST[:, hs, 0:1].broadcast_to(full3), ALU.subtract)
                        if h1 == PH:
                            ins.then_inc(best_ready, 1)

                    return [list_max, list_index, list_rest, rest_max, rest_index, all_sums,
                            lambda: sum_max(0), lambda: sum_index(0), sum_rest, lambda: sum_max(1),
                            lambda: sum_index(1), places, places_float, lambda: match(0), lambda: match(1),
                            lambda: pick(0), lambda: pick(1), lambda: add_up(0), lambda: add_up(1), experts,
                            rows_and_best]

                def gates(n):
                    dve.wait_ge(ge_ready, l * (NT + 1) + n + 1)
                    v.tensor_reduce(GSUM, GE, AX.X, ALU.add)
                    dve.drain()
                    v.reciprocal(GSUM, GSUM)
                    dve.drain()
                    v.tensor_tensor(GATE, GE, GSUM.unsqueeze(2).broadcast_to([P, PH, TOPK]), ALU.mult)
                    dve.drain()

                for half in range(2):
                    dve.wait_ge(sc_full, l * ROUTES + half + 1)
                    arrived()
                    for step in route_steps(half * PH // 2, (half + 1) * PH // 2):
                        step()
                        dve.drain()
                v.tensor_scalar(IDXV, EIDX, LOFF[:, 0:1], None, ALU.add).then_inc(idxv_ready, 1)
                gates(0)
                with dve.Fori(0, NT) as t:
                    T = dve.snap(l * NT + t)
                    rows = dve.snap(T * (USES * 16))
                    dve.drain()
                    dve.wait_ge(h_staged, l * (NT + 1) + t + 1)
                    for s in range(SLOTS):
                        dve.wait_ge(slot[s % R], rows + (s // R + 1) * 16)
                        v.tensor_tensor_reduce(out=RING[s % R], in0=RING[s % R], in1=HCUR, scale=1.0, scalar=0.0,
                                               op0=ALU.mult, op1=ALU.add, accum_out=ADOT[:, s:s + 1]).then_inc(used_dve, 1)
                    dve.drain()
                    v.memset(ACC, 0.0).then_inc(u_done, 1)
                    dve.wait_ge(gelu_done, T + 1)
                    v.tensor_tensor(WGT, AGELU, GATE.rearrange("p h k -> p (h k)"), ALU.mult).then_inc(w_ready, 1)
                    steps = route_steps()
                    for s in range(HALF - 1, SLOTS, HALF):
                        dve.drain()
                        dve.wait_ge(slot[s % R], rows + (SLOTS // R + s // R + 1) * 16)
                        v.scalar_tensor_tensor(ACC, RING[s % R], WGT[:, s:s + 1], ACC, ALU.mult, ALU.add)\
                            .then_inc(used_dve, 1)
                        k = s // HALF
                        if k == 0:
                            dve.wait_ge(sc_full, l * ROUTES + t + 3)
                            arrived()
                        if 1 <= k <= len(steps):
                            steps[k - 1]()
                    dve.drain()
                    dve.wait_ge(used_pe, T * PE_SLOTS + PE_SLOTS + 2 * PE_PER_HALF)
                    v.tensor_scalar(IDXV, EIDX, LOFF[:, 0:1], None, ALU.add).then_inc(idxv_ready, 1)
                    xt = X[:, bass.ds(t, 1), :].rearrange("p a d -> p (a d)")
                    v.tensor_tensor(ACC, ACC, YV, ALU.add).then_inc(v_taken, 1)
                    dve.drain()
                    v.tensor_tensor(xt, xt, ACC, ALU.add)
                    gates(t + 1)
                v.tensor_scalar(LOFF[:], LOFF[:], float(NEXP), None, ALU.add)
                dve.drain()
                v.memset(MX[:], 0.0).then_inc(layer_open, 1)
            dve.wait_ge(ld_gf, 16)
            dve.wait_ge(act_sq, DEPTH * (2 * NT + 1) + NT)
            v.tensor_scalar(SS[:, 0:NT], SS[:, 0:NT], 1.0 / D, EPS, ALU.mult, ALU.add).then_inc(dve_var, 1)
            dve.wait_ge(act_rt, DEPTH * 4 + 1)
            v.reciprocal(RST[:, 0:NT], RST[:, 0:NT])
            dve.drain()
            for t in range(NT):
                v.scalar_tensor_tensor(H[:, t, :], X[:, t, :], RST[:, t:t + 1], GA[:], ALU.mult, ALU.mult)\
                    .then_inc(h_ready, 1)


def shape_constants():
    import numpy as np
    f = np.float32

    def angles(pos, dim):
        inv = f(10000.0) ** (-np.arange(0, dim, 2, dtype=f) / f(dim))
        ang = pos.astype(f)[:, None] * inv[None, :].astype(f)
        return np.cos(ang).astype(f), np.sin(ang).astype(f)

    pos = np.arange(SEQ)
    c1, s1 = angles(pos, HD)
    cr, sr = angles(pos // 64, HD // 2)
    cc, sc = angles(pos % 64, HD // 2)
    cm, sm = angles(pos, 32)
    cat = lambda *a: np.concatenate(a, axis=1)
    rope = np.stack([cat(c1, c1), cat(-s1, s1), cat(cr, cr, cc, cc), cat(-sr, sr, -sc, sc)]).astype(f)
    rope_m = np.stack([cat(cm, cm), cat(-sm, sm)]).astype(f)
    rel = pos[None, :] - pos[:, None]
    window = np.where(np.abs(rel) <= 128, f(0), f(NEG))
    count = sum(((np.abs(rel) <= w // 2) & (rel % r == 0)).astype(int) for w, r in ((128, 1), (512, 4), (2048, 16)))
    dilated = np.where(count > 0, np.log(np.maximum(count, 1)) * HD ** 0.5, NEG)
    return rope, rope_m, np.stack([window, dilated]).astype(f)


def kernel(**inputs):
    import numpy as _np
    import concourse.bacc as _bacc
    from concourse import mybir as _mybir
    from concourse.bass_utils import run_bass_kernel_spmd as _run

    a = {k: _np.asarray(v) for k, v in inputs.items()}
    rope, rope_m, masks = shape_constants()

    def blocks(w, n):
        k = w.shape[1] // P
        return w.reshape(DEPTH, k, P, n, -1).transpose(0, 3, 2, 1, 4).reshape(DEPTH, n, P, -1)

    feeds = {
        "x": a["x"], "w_in": blocks(a["w_in"], ZCH), "w_out": blocks(a["w_out"], 1)[:, 0],
        "w_q": blocks(a["peer_w_q"], HC), "w_uq": blocks(a["mla_w_uq"], 1)[:, 0], "w_ukv": a["mla_w_ukv"],
        "subk": a["peer_sub_keys"].reshape(DEPTH, HC, PK, P).transpose(0, 3, 1, 2).reshape(DEPTH, P, HC * PK),
        "peer_u": a["peer_u"], "peer_v": a["peer_v"], "g_mix": a["g_mix"], "g_ffn": a["g_ffn"],
        "g_group": a["g_group"].reshape(DEPTH, D), "g_final": a["g_final"].reshape(1, D),
        "g_c": _np.concatenate([a["mla_q_norm"], a["mla_kv_norm"]], axis=1),
        "g_qk": _np.concatenate([a["ax_q_norm"], a["ax_k_norm"]], axis=1),
        "sink": a["win_sink"], "rope": rope, "rope_m": rope_m, "masks": masks,
    }
    nc = _bacc.Bacc("TRN2", target_bir_lowering=False, num_devices=1)
    arrays, args = {}, []
    for name, value in feeds.items():
        value = _np.ascontiguousarray(value)
        arrays[f"in_{name}_dram"] = value
        args.append(nc.dram_tensor(f"in_{name}_dram", value.shape, _mybir.dt.from_np(value.dtype),
                                   kind="ExternalInput").ap())
    out = nc.dram_tensor("out_0_dram", (1, SEQ, D), _mybir.dt.float32, kind="ExternalOutput").ap()
    trunk(nc, *args, out)
    r = _run(nc, [arrays], core_ids=[0])
    return r.results[0]["out_0_dram"]
```

```python
from contextlib import ExitStack

import concourse.bass as bass
from concourse import mybir

ALU = mybir.AluOpType
ACT = mybir.ActivationFunctionType
AX = mybir.AxisListType
F32 = mybir.dt.float32
U32 = mybir.dt.uint32
I32 = mybir.dt.int32

P = 128
SEQ, D = 512, 1024
DEPTH = 2
NT = SEQ // P
KD = D // P
EPS = 1e-6
HD = 64
NH = 4
GROUP_W = NH * HD
ZW = 3 * 512 + 256 + 128 + 32
GRP = 512
Z_CQ, Z_CKV, Z_KR = 1536, 1792, 1920
QKH = 6
MQ = 96
ZCH, ZC = 4, ZW // 4
NEG = -1e30
LOWEST = -3.0e38

PH, PK, TOPK = 8, 128, 16
NEXP = PK * PK
HC = 2 * PH
SLOTS = PH * TOPK
R = 8
HALF = R // 2
UH = SLOTS // HALF
USES = 2 * SLOTS // R
PE_PER_HALF = 3
NDIAG = 6
ASIDE_FROM = 2
ROUTE_FROM = 6
PE_SLOTS = SLOTS * PE_PER_HALF // HALF
WQ_SLOTS = 12
NQ0 = 4
QB = HC // NQ0
ROUTES = NT + 2
EARLY = QB // 2

HEADS = [(g, h) for g in (0, 2, 1, 3) for h in range(NH)]
UNITS = len(HEADS) * NT
MASKED = 2 * NH * NT
AHEAD = 3
BANKS = 3
MLA_AT = 13
LATENTS = 32 - 8


OUT_STEPS = [("out", 0), ("hT2", 0), ("q0",), ("out", 1), ("out", 2), ("hT2", 1), ("out", 3), ("hT2", 2), ("hT2", 3)]
NORM_STEPS = [("hT", 0), ("hT", 1), ("z", 0), ("hT", 2), ("z", 1), ("hT", 3)] + [("z", i) for i in range(2, ZCH * NT)]
ROOT_B, ROOT_C, ROOT_G, ROOT_2, ROOTS = NT, NT + 1, NT + 2, NT + 6, 2 * NT + 6
SUMS_OF_SQUARES = 2 * NT + 4

GROUP_STEPS = {2: "squares", 4: "variance", 5: "root", 7: "norm", 10: "turn"}


def group_step(u):
    p, step = u // (NH * NT) - 1, GROUP_STEPS.get(u % (NH * NT))
    return (step, p) if p >= 0 else (None, p)


def group_blocks(p):
    g = HEADS[p * NH][0]
    return 2 * g, 2 * g + 1



def key_tiles(u):
    g, t = HEADS[u // NT][0], u % NT
    return range(max(0, t - 1), min(NT, t + 2)) if g == 0 else range(NT)


def psum_jobs():
    jobs = []

    def two(kind, n, start=0):
        for i in range(n):
            jobs.append(((kind, i), "ACT" if (i + start) % 2 == 0 else "DVE"))

    for kind, i in NORM_STEPS:
        if kind == "hT":
            jobs += [(("hT", 2 * i), "ACT"), (("hT", 2 * i + 1), "ACT")]
        else:
            jobs.append(((kind, i), "DVE" if i % 2 else "ACT"))

    def qk(i):
        g, h = HEADS[i]
        jobs.append((("qT", i), "ACT"))
        if g == 3 or h % 2 == 0:
            jobs.append((("kT", i), "DVE"))

    qk(0)
    for u in range(UNITS):
        if u % NT == 0 and u // NT + 1 < len(HEADS):
            qk(u // NT + 1)
        if u == MLA_AT:
            two("cT", 3, 1)
        elif u == MLA_AT + 1:
            two("qu", NT)
        elif u == MLA_AT + 2:
            two("kv", NT)
        if group_step(u)[0] == "turn":
            a, b = group_blocks(group_step(u)[1])
            jobs += [(("yT", a), "ACT"), (("yT", b), "DVE")]
        jobs.append((("pT", u), "ACT" if u % 2 else "DVE"))
    a, b = group_blocks(3)
    jobs += [(("yT", a), "ACT"), (("yT", b), "DVE")]
    for step in OUT_STEPS:
        if step[0] == "q0":
            for i in range(NQ0):
                jobs.append((("q0", i), "ACT"))
        else:
            kind, t = step
            for i in (2 * t, 2 * t + 1):
                jobs.append(((kind, i), "ACT" if kind == "hT2" else "DVE"))
    for i in range(HC):
        jobs.append((("qry", i), "ACT"))
    return jobs


JOBS = psum_jobs()
NJ = len(JOBS)
ENG = {name: e for name, e in JOBS}
INDEX = {name: i for i, (name, _) in enumerate(JOBS)}
ORD = {}
COUNT = {"ACT": 0, "DVE": 0}
for _name, _e in JOBS:
    ORD[_name] = COUNT[_e]
    COUNT[_e] += 1


def trunk(nc, x, w_in, w_out, w_q, w_uq, w_ukv, subk, peer_u, peer_v, g_mix, g_ffn, g_group, g_final, g_c, g_qk,
          sink, rope, rope_m, masks, out):
    with ExitStack() as ctx:
        def sb(name, shape, dt=F32):
            return ctx.enter_context(nc.sbuf_tensor(name, shape, dt))

        def sem(name):
            return ctx.enter_context(nc.semaphore(name))

        X = sb("X", [P, NT, D])
        H = sb("H", [P, NT, D])
        HT = sb("HT", [P, KD, SEQ])
        WB = sb("WB", [P, WQ_SLOTS * D])
        QRY = sb("QRY", [P, HC, SEQ])
        SH = sb("SH", [P, NT * ZW + 3 * NT * SEQ])
        GA = sb("GA", [P, D])
        GG = sb("GG", [P, D])
        GC = sb("GC", [P, 384])
        GQK = sb("GQK", [P, 2, HD])
        SK = sb("SK", [P, NH])
        ROPE = sb("ROPE", [P, 4, NT, HD])
        ROPM = sb("ROPM", [P, 2, NT, 32])
        ID = sb("ID", [P, P])
        IOTI = sb("IOTI", [P, TOPK], I32)
        IOT = sb("IOT", [P, TOPK])
        LOFF = sb("LOFF", [P, 1])
        TICK = sb("TICK", [P, 1])
        SS = sb("SS", [P, 32])
        RST = sb("RST", [P, 32])
        NSK = sb("NSK", [P, NH])
        NM = sb("NM", [P, 2, NT])
        RS = sb("RS", [P, 2, NT])
        RI = sb("RI", [P, 2, NT])
        SE = sb("SE", [P, 2, NT])
        QT = sb("QT", [P, 2, SEQ])
        KT = sb("KT", [P, 2, SEQ])
        BK = ctx.enter_context(nc.psum_tensor("BK", [P, 8, 512], F32))

        hflat = H[:].rearrange("p t d -> p (t d)")
        QU_AT, KC_AT = 0, NT * NH * MQ
        QU = hflat[:, 0:NT * NH * MQ].rearrange("p (t n) -> p t n", t=NT)
        KC = hflat[:, NT * NH * MQ:2 * NT * NH * MQ].rearrange("p (t h n) -> p t h n", t=NT, h=NH)
        VD = hflat[:, 2 * NT * NH * MQ:2 * NT * NH * MQ + NT * GROUP_W].rearrange("p (t n) -> p t n", t=NT)
        scr = HT[:].rearrange("p k s -> p (k s)")
        SCR_M = scr[:, 0:NT * 384].rearrange("p (t n) -> p t n", t=NT)
        SQ = scr[:, 3072:4096].rearrange("p (t n) -> p t n", t=NT)
        qflat = QRY[:].rearrange("p a s -> p (a s)")
        MASK = [qflat[:, i * 2048:(i + 1) * 2048].rearrange("p (t s) -> p t s", t=NT) for i in range(2)]
        WUQ = qflat[:, 4096:4096 + 768].rearrange("p (k n) -> p k n", k=2)
        WUKV = qflat[:, 4864:4864 + 512]
        Z = SH[:, 0:NT * ZW].rearrange("p (t n) -> p t n", t=NT)
        PR = SH[:, NT * ZW:NT * ZW + 2048].rearrange("p (t s) -> p t s", t=NT)
        PT = SH[:, NT * ZW + 2048:NT * ZW + 3584].rearrange("p (b s) -> p b s", b=3)
        CT = SH[:, NT * ZW + 3584:NT * ZW + 5120].rearrange("p (b s) -> p b s", b=3)
        SCR_B = SH[:, NT * ZW:NT * ZW + NT * 384].rearrange("p (t n) -> p t n", t=NT)
        SCR_P = SH[:, NT * ZW + 3584:NT * ZW + 3584 + NT * 384].rearrange("p (t n) -> p t n", t=NT)
        KTM = SH[0:MQ, NT * ZW + 3584:NT * ZW + 4608].rearrange("p (b s) -> p b s", b=2)
        place = [0]

        def shared(n):
            place[0] += n
            return SH[:, place[0] - n:place[0]]

        SUBK = shared(2048).rearrange("p (a n) -> p a n", a=HC)
        QST = shared(2048).rearrange("p (a n) -> p a n", a=HC)
        HCUR = shared(D)
        ACC = shared(D)
        DIAG = shared(NDIAG * P).rearrange("p (n m) -> p n m", n=NDIAG)
        S12 = shared(HC * TOPK).rearrange("p (a k) -> p a k", a=HC)
        I12 = shared(HC * TOPK).bitcast(U32).rearrange("p (a k) -> p a k", a=HC)
        I12F = shared(HC * TOPK).rearrange("p (a k) -> p a k", a=HC)
        work = [shared(HC * PK), shared(HC * PK)]
        REST = work[0].rearrange("p (a n) -> p a n", a=HC)
        SUMS = work[1].rearrange("p (h n) -> p h n", h=PH)
        ONE = [w.rearrange("p (h k a) -> p h k a", h=PH, k=TOPK) for w in work]
        BEST = shared(SLOTS).rearrange("p (h k) -> p h k", h=PH)
        POS = shared(SLOTS).bitcast(U32).rearrange("p (h k) -> p h k", h=PH)
        PAB = shared(2 * SLOTS).bitcast(U32).rearrange("p (c h k) -> p c h k", c=2, h=PH)
        PABF = shared(2 * SLOTS).rearrange("p (c h k) -> p c h k", c=2, h=PH)
        ISEL = shared(2 * SLOTS).rearrange("p (c h k) -> p c h k", c=2, h=PH)
        EIDX = shared(SLOTS)
        IDXU, IDXV = shared(SLOTS).bitcast(I32), shared(SLOTS).bitcast(I32)
        GE = shared(SLOTS).rearrange("p (h k) -> p h k", h=PH)
        GATE = shared(SLOTS).rearrange("p (h k) -> p h k", h=PH)
        GSUM = shared(PH)
        ADOT = shared(SLOTS)
        AGELU = shared(SLOTS)
        WGT = shared(SLOTS)
        assert place[0] <= NT * ZW + 3 * NT * SEQ

        WZ_AT = [R * D, 0, KD * ZC, R * D]
        WZ = [WB[:, a:a + KD * ZC].rearrange("p (k n) -> p k n", k=KD) for a in WZ_AT]
        WO = qflat[:, 0:KD * D].rearrange("p (k n) -> p k n", k=KD)
        WQ = [WB[:, i * D:(i + 1) * D].rearrange("p (k n) -> p k n", k=KD) for i in range(WQ_SLOTS)]
        RING = [WB[:, i * D:(i + 1) * D] for i in range(R)]
        OUT = BK[:, 7, :].rearrange("p (t n) -> p t n", t=NT)
        SC = BK[:, 0:4, :].rearrange("p b (a n) -> p (b a) n", n=PK)
        YV = BK[:, 4:6, :].rearrange("p b n -> p (b n)")

        ld_x, ld_const = [sem(f"ld_x{t}") for t in range(NT)], sem("ld_const")
        ld_ga, ld_attn, ld_wo, ld_sub, ld_gf = sem("ld_ga"), sem("ld_attn"), sem("ld_wo"), sem("ld_sub"), sem("ld_gf")
        ld_wz = [sem(f"ld_wz{i}") for i in range(ZCH)]
        ld_wq = [sem(f"ld_wq{i}") for i in range(HC)]
        stored = sem("stored")
        ident_done, iota_done = sem("ident_done"), sem("iota_done")
        layer_open = sem("layer_open")
        psum_full = sem("psum_full")
        act_free, dve_free = sem("act_free"), sem("dve_free")
        act_sq, dve_var, act_rt = sem("act_sq"), sem("dve_var"), sem("act_rt")
        h_ready, c_ready = sem("h_ready"), sem("c_ready")
        qkd_ready, b_ready, ac_ready = sem("qkd_ready"), sem("b_ready"), sem("ac_ready")
        s_full, s_max, p_ready, y_ready = sem("s_full"), sem("s_max"), sem("p_ready"), sem("y_ready")
        o_full, o_free = sem("o_full"), sem("o_free")
        q_staged, h_staged, sc_full, sc_used = sem("q_staged"), sem("h_staged"), sem("sc_full"), sem("sc_used")
        best_ready, ge_ready = sem("best_ready"), sem("ge_ready")
        idxu_ready, idxv_ready = sem("idxu_ready"), sem("idxv_ready")
        slot = [sem(f"slot{i}") for i in range(R)]
        used_dve, used_pe = sem("used_dve"), sem("used_pe")
        u_done, gelu_done, w_ready = sem("u_done"), sem("gelu_done"), sem("w_ready")
        diag_ready, v_done, v_taken = sem("diag_ready"), sem("v_done"), sem("v_taken")

        table_u = peer_u.rearrange("l n d -> (l n) d")
        table_v = peer_v.rearrange("l n d -> (l n) d")

        def bank(name):
            return 4 + INDEX[name] % BANKS

        def freed(eng, l, name):
            s = act_free if ENG[name] == "ACT" else dve_free
            eng.wait_ge(s, l * COUNT[ENG[name]] + ORD[name] + 1)

        def full(eng, l, name):
            eng.wait_ge(psum_full, l * NJ + INDEX[name] + 1)

        block = ctx.enter_context(nc.Block())

        @block.sync
        def _(sp):
            sp.dma_start(X[:, 0, :], x[0, 0:P, :]).then_inc(ld_x[0], 16)
            sp.dma_start(GA[:], g_mix[0:1].broadcast_to([P, D])).then_inc(ld_ga, 16)
            sp.dma_start(X[:, 1, :], x[0, P:2 * P, :]).then_inc(ld_x[1], 16)
            sp.dma_start(WB[:, WZ_AT[0]:WZ_AT[0] + KD * ZC], w_in[0, 0]).then_inc(ld_wz[0], 16)
            for t in range(2, NT):
                sp.dma_start(X[:, t, :], x[0, t * P:(t + 1) * P, :]).then_inc(ld_x[t], 16)
            sp.wait_ge(ld_ga, 16)
            sp.wait_ge(ld_wz[0], 16)
            for i in range(4):
                sp.dma_start(ROPE[:, i], rope[i].rearrange("(t p) n -> p t n", p=P)).then_inc(ld_const, 16)
            for i in range(2):
                sp.dma_start(ROPM[:, i], rope_m[i].rearrange("(t p) n -> p t n", p=P)).then_inc(ld_const, 16)
            with sp.Fori(0, DEPTH) as l:
                sp.wait_ge(layer_open, l + 1)
                for c in (1, 2):
                    sp.dma_start(WB[:, WZ_AT[c]:WZ_AT[c] + KD * ZC], w_in[l, c]).then_inc(ld_wz[c], 16)
                sp.dma_start(GG[:], g_group[bass.ds(l, 1)].broadcast_to([P, D])).then_inc(ld_attn, 16)
                sp.dma_start(GC[:], g_c[bass.ds(l, 1)].broadcast_to([P, 384])).then_inc(ld_attn, 16)
                sp.dma_start(GQK[:].rearrange("p a n -> p (a n)"),
                             g_qk[bass.ds(l, 1)].broadcast_to([P, 2 * HD])).then_inc(ld_attn, 16)
                sp.dma_start(SK[:], sink[bass.ds(l, 1)].broadcast_to([P, NH])).then_inc(ld_attn, 16)
                for i in range(2):
                    sp.dma_start(MASK[i], masks[i].rearrange("(t p) s -> p t s", p=P)).then_inc(ld_attn, 16)
                sp.dma_start(qflat[:, 4096:4096 + 768], w_uq[l]).then_inc(ld_attn, 16)
                sp.dma_start(WUKV, w_ukv[l]).then_inc(ld_attn, 16)
                full(sp, l, ("z", NT - 1))
                sp.dma_start(WB[:, WZ_AT[3]:WZ_AT[3] + KD * ZC], w_in[l, 3]).then_inc(ld_wz[3], 16)
                full(sp, l, ("z", ZCH * NT - 1))
                for i in range(WQ_SLOTS):
                    s = (i + R) % WQ_SLOTS
                    sp.dma_start(WB[:, s * D:(s + 1) * D], w_q[l, i]).then_inc(ld_wq[i], 16)
                sp.wait_ge(h_ready, l * 2 * NT + NT)
                sp.dma_start(GA[:], g_ffn[bass.ds(l, 1)].broadcast_to([P, D])).then_inc(ld_ga, 16)
                full(sp, l, ("pT", MASKED - 1))
                sp.dma_start(qflat[:, 0:KD * D], w_out[l]).then_inc(ld_wo, 16)
                full(sp, l, ("yT", group_blocks(3)[1]))
                sp.dma_start(SH[:, 0:HC * PK], subk[l]).then_inc(ld_sub, 16)
                full(sp, l, ("q0", 0))
                for i in range(WQ_SLOTS, HC):
                    s = (i + R) % WQ_SLOTS
                    sp.dma_start(WB[:, s * D:(s + 1) * D], w_q[l, i]).then_inc(ld_wq[i], 16)
                nxt = sp.snap((l + 1) % DEPTH)
                sp.wait_ge(h_ready, (l + 1) * 2 * NT)
                sp.dma_start(GA[:], g_mix[bass.ds(nxt, 1)].broadcast_to([P, D])).then_inc(ld_ga, 16)
                for i in range(HC - QB):
                    full(sp, l, ("qry", i))
                    s = R + i % QB
                    sp.dma_start(WB[:, s * D:(s + 1) * D], w_q[l, i]).then_inc(ld_wq[i], 16)
                full(sp, l, ("qry", HC - 1))
                sp.dma_start(WB[:, WZ_AT[0]:WZ_AT[0] + KD * ZC], w_in[nxt, 0]).then_inc(ld_wz[0], 16)
            sp.wait_ge(layer_open, DEPTH + 1)
            sp.wait_ge(ld_ga, DEPTH * 32 + 16)
            sp.wait_ge(ld_wz[0], (DEPTH + 1) * 16)
            sp.dma_start(GA[:], g_final.broadcast_to([P, D])).then_inc(ld_gf, 16)
            for t in range(NT):
                sp.wait_ge(h_ready, DEPTH * 2 * NT + t + 1)
                sp.dma_start(out[0, t * P:(t + 1) * P, :], H[:, t, :]).then_inc(stored, 16)
            sp.wait_ge(stored, 16 * NT)

        @block.gpsimd
        def _(pool):
            dve_need, pe_need = pool.alloc_register("dve_need"), pool.alloc_register("pe_need")
            u_need, v_need = pool.alloc_register("u_need"), pool.alloc_register("v_need")
            nc.gpsimd.memset(ID[:], 0.0)
            pool.drain()
            nc.gpsimd.affine_select(out=ID[:], in_=ID[:], compare_op=ALU.not_equal, fill=1.0, base=0,
                                    pattern=[[-1, P]], channel_multiplier=1).then_inc(ident_done, 1)
            nc.gpsimd.iota(IOTI[:], [[1, TOPK]], base=0, channel_multiplier=0).then_inc(iota_done, 1)
            pool.wait_ge(ld_const, 16 * 6)
            pool.reg_mov(dve_need, 1)
            pool.reg_mov(pe_need, PE_PER_HALF)
            pool.reg_mov(u_need, 1)
            pool.reg_mov(v_need, 1)
            with pool.Fori(0, DEPTH) as l:
                for g in (0, 2):
                    last = NT if g == 0 else ZCH * NT
                    freed(pool, l, ("z", last - 2))
                    freed(pool, l, ("z", last - 1))
                    zz = Z[:, :, g * GRP:g * GRP + QKH * HD].rearrange("p t (h n) -> p t h n", n=HD)
                    sc = SCR_P.rearrange("p t (h n) -> p t h n", n=HD)
                    cos = ROPE[:, 0].unsqueeze(2).broadcast_to([P, NT, QKH, HD])
                    sin = ROPE[:, 1].unsqueeze(2).broadcast_to([P, NT, QKH, HD])
                    nc.gpsimd.tensor_tensor(sc[:, :, :, 0:32], zz[:, :, :, 32:64], sin[:, :, :, 0:32], ALU.mult)
                    nc.gpsimd.tensor_tensor(sc[:, :, :, 32:64], zz[:, :, :, 0:32], sin[:, :, :, 32:64], ALU.mult)
                    pool.drain()
                    nc.gpsimd.tensor_tensor(zz, zz, cos, ALU.mult)
                    pool.drain()
                    nc.gpsimd.tensor_tensor(zz, zz, sc, ALU.add).then_inc(ac_ready, 1)
                    pool.drain()

                def ring_free(k):
                    v_before = k < 2 or k >= UH + 2
                    pool.wait_ge(used_dve, dve_need)
                    pool.reg_add(dve_need, dve_need, HALF if 1 <= k <= UH else 1)
                    if v_before:
                        pool.wait_ge(used_pe, pe_need)
                        pool.reg_add(pe_need, pe_need, PE_PER_HALF)

                def gather(table, idx, s):
                    nc.gpsimd.indirect_dma_start(
                        out=RING[s % R], out_offset=None, in_=table,
                        in_offset=bass.IndirectOffsetOnAxis(ap=idx[:, s:s + 1], axis=0)).then_inc(slot[s % R], 16)

                with pool.Fori(0, NT) as t:
                    pool.wait_ge(idxu_ready, u_need)
                    pool.reg_add(u_need, u_need, 1)
                    for s in range(SLOTS):
                        if s == EARLY * TOPK:
                            pool.wait_ge(idxu_ready, u_need)
                            pool.reg_add(u_need, u_need, 1)
                        if s % HALF == 0:
                            ring_free(s // HALF)
                        gather(table_u, IDXU, s)
                    pool.wait_ge(idxv_ready, v_need)
                    pool.reg_add(v_need, v_need, 1)
                    for s in range(SLOTS):
                        if s % HALF == 0:
                            ring_free(UH + s // HALF)
                        gather(table_v, IDXV, s)
                pool.reg_add(u_need, u_need, 2)

        @block.tensor
        def _(pe):
            pe.wait_ge(ident_done, 1)
            with pe.Fori(0, DEPTH) as l:
                def begin(name):
                    i = INDEX[name]
                    if i >= BANKS:
                        freed(pe, l, JOBS[i - BANKS][0])
                    return BK[:, bank(name), :]

                def norm_turned(kind, t, n_ready):
                    for n in range(2):
                        b = begin((kind, 2 * t + n))
                        if n == 0:
                            pe.wait_ge(h_ready, l * 2 * NT + n_ready)
                        for m in range(KD // 2):
                            k = n * KD // 2 + m
                            ins = nc.tensor.transpose(b[:, m * P:(m + 1) * P], H[:, t, k * P:(k + 1) * P], ID[:])
                        ins.then_inc(psum_full, 1)

                for kind, i in NORM_STEPS:
                    if kind == "hT":
                        norm_turned("hT", i, i + 1)
                        continue
                    c, t = i // NT, i % NT
                    if t == 0:
                        pe.wait_ge(ld_wz[c], (l + 1) * 16)
                    b = begin(("z", i))
                    if c == 0:
                        freed(pe, l, ("hT", 2 * t + 1))
                    for k in range(KD):
                        ins = nc.tensor.matmul(b[:, 0:ZC], HT[:, k, t * P:(t + 1) * P], WZ[c][:, k, :],
                                               start=(k == 0), stop=(k == KD - 1))
                    ins.then_inc(psum_full, 1)
                pe.wait_ge(ld_attn, (l + 1) * 16 * 8)

                def latents_turned():
                    pe.wait_ge(c_ready, l + 1)
                    pe.wait_ge(ac_ready, (l + 1) * 2)
                    for k in range(3):
                        b = begin(("cT", k))
                        for t in range(NT):
                            ins = nc.tensor.transpose(b[:, t * P:(t + 1) * P],
                                                      Z[:, t, Z_CQ + k * P:Z_CQ + (k + 1) * P], ID[:])
                        ins.then_inc(psum_full, 1)

                def latent_queries():
                    freed(pe, l, ("cT", 0))
                    freed(pe, l, ("cT", 1))
                    for t in range(NT):
                        b = begin(("qu", t))
                        for k in range(2):
                            ins = nc.tensor.matmul(b[:, 0:NH * MQ], CT[:, k, t * P:(t + 1) * P], WUQ[:, k, :],
                                                   start=(k == 0), stop=(k == 1))
                        ins.then_inc(psum_full, 1)

                def latent_keys():
                    freed(pe, l, ("cT", 2))
                    for t in range(NT):
                        b = begin(("kv", t))
                        nc.tensor.matmul(b, CT[:, 2, t * P:(t + 1) * P], WUKV, start=True, stop=True)\
                            .then_inc(psum_full, 1)

                def queries(i):
                    g, h = HEADS[i]
                    if h == 0:
                        if g == 1:
                            pe.wait_ge(b_ready, l + 1)
                        elif g == 3:
                            pe.wait_ge(qkd_ready, l + 1)
                        else:
                            pe.wait_ge(ac_ready, l * 2 + (1 if g == 0 else 2))
                    b = begin(("qT", i))
                    for t in range(NT):
                        q = QU_AT + (t * NH + h) * MQ
                        src = hflat[:, q:q + P] if g == 3 else Z[:, t, g * GRP + h * HD:g * GRP + h * HD + P]
                        ins = nc.tensor.transpose(b[:, t * P:(t + 1) * P], src, ID[:])
                    ins.then_inc(psum_full, 1)
                    if ("kT", i) in INDEX:
                        b = begin(("kT", i))
                        for t in range(NT):
                            c = g * GRP + GROUP_W + h // 2 * HD
                            k = KC_AT + (t * NH + h) * MQ
                            src = hflat[:, k:k + P] if g == 3 else Z[:, t, c:c + P]
                            ins = nc.tensor.transpose(b[:, t * P:(t + 1) * P], src, ID[:])
                        ins.then_inc(psum_full, 1)

                def scores(u):
                    i, t = u // NT, u % NT
                    g, h = HEADS[i]
                    w = MQ if g == 3 else P
                    keys = KTM[:, h % 2, :] if g == 3 else KT[:, (h // 2) % 2, :]
                    if t == 0:
                        freed(pe, l, ("qT", i))
                        if ("kT", i) in INDEX:
                            freed(pe, l, ("kT", i))
                    if u >= NT:
                        if HEADS[(u - NT) // NT][0] in (0, 2):
                            pe.wait_ge(s_max, l * UNITS + u - NT + 1)
                        else:
                            pe.wait_ge(p_ready, l * UNITS + u - NT + 1)
                    ks = slice(key_tiles(u)[0] * P, (key_tiles(u)[-1] + 1) * P)
                    nc.tensor.matmul(BK[:, t, ks], QT[0:w, i % 2, t * P:(t + 1) * P], keys[:, ks],
                                     start=True, stop=True).then_inc(s_full, 1)

                def turn(u):
                    pe.wait_ge(p_ready, l * UNITS + u + 1)
                    b = begin(("pT", u))
                    for kt in key_tiles(u):
                        ins = nc.tensor.transpose(b[:, kt * P:(kt + 1) * P], PR[:, u % NT, kt * P:(kt + 1) * P], ID[:])
                    ins.then_inc(psum_full, 1)

                def product(u):
                    i, t = u // NT, u % NT
                    g, h = HEADS[i]
                    freed(pe, l, ("pT", u))
                    if t == 0:
                        pe.wait_ge(o_free, l * len(HEADS) + i + 1)
                    for kt in key_tiles(u):
                        c = g * GRP + GROUP_W + 2 * HD
                        v = VD[:, kt, h // 2 * P:h // 2 * P + P] if g == 3 else Z[:, kt, c:c + P]
                        ins = nc.tensor.matmul(OUT[:, t, :], PT[:, u % 3, kt * P:(kt + 1) * P], v,
                                               start=(kt == key_tiles(u)[0]), stop=(kt == key_tiles(u)[-1]))
                    ins.then_inc(o_full, 1)

                def group_turned(p):
                    pe.wait_ge(y_ready, l * 4 + p + 1)
                    for k in group_blocks(p):
                        b = begin(("yT", k))
                        for t in range(NT):
                            c = k // 2 * GRP + k % 2 * P
                            ins = nc.tensor.transpose(b[:, t * P:(t + 1) * P], Z[:, t, c:c + P], ID[:])
                        ins.then_inc(psum_full, 1)

                queries(0)
                for u in range(AHEAD):
                    scores(u)
                for u in range(UNITS):
                    if u % NT == 0 and u // NT + 1 < len(HEADS):
                        queries(u // NT + 1)
                    if u + AHEAD < UNITS:
                        scores(u + AHEAD)
                    if MLA_AT <= u < MLA_AT + 3:
                        (latents_turned, latent_queries, latent_keys)[u - MLA_AT]()
                    if group_step(u)[0] == "turn":
                        group_turned(group_step(u)[1])
                    turn(u)
                    if u > 0:
                        product(u - 1)
                product(UNITS - 1)

                group_turned(3)
                for k in group_blocks(3):
                    freed(pe, l, ("yT", k))
                pe.wait_ge(ld_wo, (l + 1) * 16)

                def project(t):
                    for n in range(2):
                        b = begin(("out", 2 * t + n))
                        for k in range(KD):
                            ins = nc.tensor.matmul(b, HT[:, k, t * P:(t + 1) * P], WO[:, k, n * 512:(n + 1) * 512],
                                                   start=(k == 0), stop=(k == KD - 1))
                        ins.then_inc(psum_full, 1)

                def key_scores(lists):
                    for a in lists:
                        ins = nc.tensor.matmul(SC[:, a, :], QST[:, a, :], SUBK[:, a, :], start=True, stop=True)
                    ins.then_inc(sc_full, 1)

                def first_queries():
                    freed(pe, l, ("hT2", 0))
                    freed(pe, l, ("hT2", 1))
                    for i in range(NQ0):
                        b = begin(("q0", i))
                        for m in range(QB):
                            a = i * QB + m
                            pe.wait_ge(ld_wq[a], l * (32 if a < HC - QB else 16) + 16)
                            for k in range(KD):
                                ins = nc.tensor.matmul(b[:, m * P:(m + 1) * P], WQ[(a + R) % WQ_SLOTS][:, k, :],
                                                       HT[:, k, 0:P], start=(k == 0), stop=(k == KD - 1))
                        ins.then_inc(psum_full, 1)
                        if i == 0:
                            pe.wait_ge(ld_sub, (l + 1) * 16)
                            freed(pe, l, ("q0", 0))
                            key_scores(range(QB))
                    freed(pe, l, ("q0", NQ0 - 1))
                    key_scores(range(QB, HC))

                for step in OUT_STEPS:
                    if step[0] == "out":
                        project(step[1])
                    elif step[0] == "hT2":
                        norm_turned("hT2", step[1], NT + step[1] + 1)
                    else:
                        first_queries()
                freed(pe, l, ("hT2", 2 * NT - 2))
                freed(pe, l, ("hT2", 2 * NT - 1))
                for i in range(HC):
                    a = (i + HC - QB) % HC
                    b = begin(("qry", i))
                    if i >= QB:
                        pe.wait_ge(ld_wq[a], (l + 1) * 32)
                    for k in range(KD):
                        ins = nc.tensor.matmul(b[:, 0:SEQ - P], WQ[R + i % QB][:, k, :], HT[:, k, P:SEQ],
                                               start=(k == 0), stop=(k == KD - 1))
                    ins.then_inc(psum_full, 1)
                with pe.Fori(0, NT) as t:
                    T = pe.snap(l * NT + t)
                    pe.wait_ge(sc_used, l * ROUTES + t + 2)
                    pe.wait_ge(q_staged, T + 1)
                    key_scores(range(HC))
                    rows = pe.snap(T * (USES * 16))
                    diags = pe.snap(T * PE_SLOTS)
                    pe.wait_ge(v_taken, T + 1)
                    freed(pe, l, ("qry", HC - 1))
                    n = 0
                    for s in range(SLOTS):
                        if s % HALF == HALF - 1:
                            continue
                        pe.wait_ge(diag_ready, diags + (n + 1))
                        pe.wait_ge(slot[s % R], rows + (SLOTS // R + s // R + 1) * 16)
                        for b in range(2):
                            ins = nc.tensor.matmul(BK[:, 4 + b, :], DIAG[:, n % NDIAG, :],
                                                   RING[s % R][:, b * 512:(b + 1) * 512],
                                                   start=(n == 0), stop=(n == PE_SLOTS - 1))
                        ins.then_inc(used_pe, 1)
                        n += 1

        @block.scalar
        def _(act):
            def copy_out(l, name, dst, src):
                full(act, l, name)
                nc.scalar.copy(dst, src).then_inc(act_free, 1)

            def squares(t):
                nc.scalar.activation(H[:, t, :], X[:, t, :], ACT.Square, accum_out=SS[:, t:t + 1]).then_inc(act_sq, 1)

            def root(l, n, cols, at=0):
                act.wait_ge(dve_var, l * ROOTS + n + 1)
                nc.scalar.activation(RST[:, at:at + cols], SS[:, at:at + cols], ACT.Sqrt).then_inc(act_rt, 1)

            act.wait_ge(ident_done, 1)
            with act.Fori(0, DEPTH) as l:
                act.wait_ge(layer_open, l + 1)

                def norm_out(kind, t):
                    for n in range(2):
                        copy_out(l, (kind, 2 * t + n), HT[:, n * KD // 2:(n + 1) * KD // 2, t * P:(t + 1) * P],
                                 BK[:, bank((kind, 2 * t + n)), :].rearrange("p (k n) -> p k n", n=P))

                def projected(i):
                    c, t = i // NT, i % NT
                    copy_out(l, ("z", i), Z[:, t, c * ZC:(c + 1) * ZC], BK[:, bank(("z", i)), 0:ZC])

                for t in range(NT):
                    act.wait_ge(ld_x[t], 16)
                    squares(t)
                    root(l, t, 1, t)
                    if 1 <= t < NT - 1:
                        norm_out("hT", t - 1)
                projected(0)
                norm_out("hT", NT - 2)
                norm_out("hT", NT - 1)
                for i in range(2, ZCH * NT, 2):
                    projected(i)
                    if i == 2 * NT + 2:
                        root(l, ROOT_B, LATENTS)

                def latents(u):
                    if u == MLA_AT:
                        copy_out(l, ("cT", 1), CT[:, 1, :], BK[:, bank(("cT", 1)), :])
                    if u == MLA_AT + 1:
                        for t in range(0, NT, 2):
                            copy_out(l, ("qu", t), QU[:, t, :], BK[:, bank(("qu", t)), 0:NH * MQ])
                    if u == MLA_AT + 2:
                        for t in range(0, NT, 2):
                            kv = BK[:, bank(("kv", t)), :].rearrange("p (h n) -> p h n", h=NH)
                            full(act, l, ("kv", t))
                            nc.scalar.copy(KC[:, t, :, 0:HD], kv[:, :, 0:HD])
                            nc.scalar.copy(VD[:, t, :].rearrange("p (h n) -> p h n", h=NH), kv[:, :, HD:2 * HD])\
                                .then_inc(act_free, 1)

                def queries(i):
                    w = MQ if HEADS[i][0] == 3 else P
                    scale = {0: 1.0, 1: HD ** -0.5, 2: 1.0, 3: MQ ** -0.5}[HEADS[i][0]]
                    full(act, l, ("qT", i))
                    nc.scalar.activation(QT[0:w, i % 2, :], BK[0:w, bank(("qT", i)), :], ACT.Copy, scale=scale)\
                        .then_inc(act_free, 1)

                def probs(u):
                    i, t = u // NT, u % NT
                    g, h = HEADS[i]
                    act.wait_ge(s_max, l * UNITS + u + 1)
                    if u >= NT:
                        full(act, l, ("pT", u - NT))
                    bias = NM[:, i % 2, t:t + 1]
                    rows = RS[:, i % 2, t:t + 1]
                    if g in (0, 2):
                        ks = slice(key_tiles(u)[0] * P, (key_tiles(u)[-1] + 1) * P)
                        ins = nc.scalar.activation(PR[:, t, ks], PR[:, t, ks], ACT.Exp, bias=bias, scale=-1.0,
                                                   accum_out=rows)
                    else:
                        ins = nc.scalar.activation(PR[:, t, :], BK[:, t, :], ACT.Exp, bias=bias, accum_out=rows)
                    if g == 0 and t == NT - 1:
                        ins = nc.scalar.activation(SE[:, i % 2, :], NM[:, i % 2, :], ACT.Exp, bias=SK[:, h:h + 1])
                    ins.then_inc(p_ready, 1)

                def group(step, p):
                    if step == "squares":
                        act.wait_ge(o_free, l * len(HEADS) + (p + 1) * NH + 1)
                        z = HEADS[p * NH][0] * GRP
                        for t in range(NT):
                            ins = nc.scalar.activation(SQ[:, t, :], Z[:, t, z:z + GROUP_W], ACT.Square,
                                                       accum_out=SS[:, 4 * p + t:4 * p + t + 1])
                        ins.then_inc(act_sq, 1)
                    if step == "root":
                        root(l, ROOT_G + p, 4, 4 * p)
                    if step == "turn":
                        k = group_blocks(p)[0]
                        copy_out(l, ("yT", k), HT[:, k, :], BK[:, bank(("yT", k)), :])

                act.wait_ge(ld_attn, (l + 1) * 16 * 8)
                queries(0)
                for u in range(AHEAD - 1):
                    probs(u)
                for u in range(UNITS):
                    if u % NT == 0 and u // NT + 1 < len(HEADS):
                        queries(u // NT + 1)
                    if u + AHEAD - 1 < UNITS:
                        probs(u + AHEAD - 1)
                    if u == 4:
                        root(l, ROOT_C, 8, LATENTS)
                    latents(u)
                    group(*group_step(u))
                    if u % 2:
                        if u >= 3:
                            act.wait_ge(o_full, l * UNITS + u - 2)
                        ks = slice(key_tiles(u)[0] * P, (key_tiles(u)[-1] + 1) * P)
                        copy_out(l, ("pT", u), PT[:, u % 3, ks], BK[:, bank(("pT", u)), ks])
                for step in ("squares", "root", "turn"):
                    group(step, 3)
                def second_norm(t):
                    freed(act, l, ("out", 2 * t + 1))
                    squares(t)
                    root(l, ROOT_2 + t, 1, t)

                second_norm(0)
                norm_out("hT2", 0)
                for i in range(NQ0):
                    copy_out(l, ("q0", i), QST[:, i * QB:(i + 1) * QB, :].rearrange("p a n -> p (a n)"),
                             BK[:, bank(("q0", i)), :])

                def queries_out(n):
                    for i in n:
                        copy_out(l, ("qry", i), QRY[:, (i + HC - QB) % HC, P:SEQ],
                                 BK[:, bank(("qry", i)), 0:SEQ - P])

                act.wait_ge(h_ready, l * 2 * NT + NT + 1)
                nc.scalar.copy(HCUR, H[:, 0, :]).then_inc(h_staged, 1)
                second_norm(1)
                second_norm(2)
                norm_out("hT2", 1)
                second_norm(3)
                norm_out("hT2", 2)
                norm_out("hT2", 3)
                act.wait_ge(best_ready, l * (NT + 1) + 1)
                nc.scalar.activation(GE, GE, ACT.Exp).then_inc(ge_ready, 1)
                act.wait_ge(h_ready, (l + 1) * 2 * NT)
                queries_out(range(HC))
                act.drain()
                with act.Fori(0, NT) as t:
                    T = act.snap(l * NT + t)
                    nxt = act.snap(t % (NT - 1) + 1)
                    act.wait_ge(sc_full, l * ROUTES + t + 2)
                    nc.scalar.copy(QST, QRY[:, :, bass.ds(nxt * P, P)]).then_inc(q_staged, 1)
                    act.wait_ge(u_done, T + 1)
                    nc.scalar.activation(AGELU, ADOT, ACT.Gelu).then_inc(gelu_done, 1)
                    nc.scalar.copy(HCUR, H[:, bass.ds(nxt, 1), :].rearrange("p a d -> p (a d)")).then_inc(h_staged, 1)
                    used = act.snap(T * PE_SLOTS + PE_PER_HALF * 2)
                    act.wait_ge(w_ready, T + 1)
                    n = 0
                    for s in range(SLOTS):
                        if s % HALF == HALF - 1:
                            continue
                        if n % PE_PER_HALF == 0:
                            act.wait_ge(used_pe, used + (n - NDIAG + PE_PER_HALF))
                        nc.scalar.activation(DIAG[:, n % NDIAG, :], ID[:], ACT.Copy,
                                             scale=WGT[:, s:s + 1]).then_inc(diag_ready, 1)
                        n += 1
                    act.wait_ge(best_ready, l * (NT + 1) + t + 2)
                    nc.scalar.activation(GE, GE, ACT.Exp).then_inc(ge_ready, 1)
            act.wait_ge(layer_open, DEPTH + 1)
            squares(0)
            for t in range(NT):
                if t + 1 < NT:
                    squares(t + 1)
                root(DEPTH, t, 1, t)

        @block.vector
        def _(dve):
            v = nc.vector

            def arrived():
                v.tensor_copy(TICK[:], LOFF[:])
                dve.drain()

            def copy_out(l, name, dst, src):
                full(dve, l, name)
                v.tensor_copy(dst, src).then_inc(dve_free, 1)

            def variances(widths, at=0):
                for cols, width in widths:
                    ins = v.tensor_scalar(SS[:, at:at + cols], SS[:, at:at + cols], 1.0 / width, EPS, ALU.mult, ALU.add)
                    at += cols
                ins.then_inc(dve_var, 1)

            def inverse(l, n, cols, at=0):
                dve.wait_ge(act_rt, l * ROOTS + n + 1)
                v.reciprocal(RST[:, at:at + cols], RST[:, at:at + cols])
                dve.drain()

            def variance(l, n, t):
                dve.wait_ge(act_sq, l * SUMS_OF_SQUARES + n + 1)
                variances([(1, D)], t)

            def normalise(l, n, t):
                inverse(l, n, 1, t)
                v.scalar_tensor_tensor(H[:, t, :], X[:, t, :], RST[:, t:t + 1], GA[:], ALU.mult, ALU.mult)\
                    .then_inc(h_ready, 1)

            v.memset(LOFF[:], 0.0)
            v.memset(KT[:], 0.0)
            v.memset(NSK[:], 0.0).then_inc(used_dve, 2)
            v.memset(NM[:], 0.0).then_inc(used_pe, 2 * PE_PER_HALF)
            v.memset(RI[:], 0.0).then_inc(v_taken, 1)
            v.memset(RS[:], 0.0).then_inc(o_free, 1)
            v.memset(SS[:], 0.0).then_inc(layer_open, 1)
            dve.wait_ge(iota_done, 1)
            v.tensor_copy(IOT[:], IOTI[:])
            dve.drain()
            with dve.Fori(0, DEPTH) as l:
                for t in range(NT):
                    variance(l, t, t)
                    if t == 0:
                        dve.wait_ge(ld_ga, l * 32 + 16)
                    normalise(l, t, t)
                zb = Z[:, :, GRP:GRP + QKH * HD]
                zbh = zb.rearrange("p t (h n) -> p t h n", n=HD)
                zc = Z[:, :, Z_CQ:Z_CQ + 384]
                sh = SCR_B.rearrange("p t (h n) -> p t h n", n=HD)

                def b_squares():
                    freed(dve, l, ("z", 2 * NT - 2))
                    v.tensor_tensor(SCR_B, zb, zb, ALU.mult)
                    dve.drain()
                    v.tensor_reduce(SS[:, 0:LATENTS].rearrange("p (t h) -> p t h", t=NT), sh, AX.X, ALU.add)
                    dve.drain()
                    variances([(LATENTS, HD)])

                def b_norm():
                    inverse(l, ROOT_B, LATENTS)
                    rb = RST[:, 0:LATENTS].rearrange("p (t h) -> p t h", t=NT).unsqueeze(3)\
                        .broadcast_to([P, NT, QKH, HD])
                    v.tensor_tensor(zbh, zbh, rb, ALU.mult)
                    dve.drain()
                    for a, (h0, h1) in enumerate(((0, NH), (NH, QKH))):
                        gain = GQK[:, a, :].unsqueeze(1).unsqueeze(1).broadcast_to([P, NT, h1 - h0, HD])
                        v.tensor_tensor(zbh[:, :, h0:h1, :], zbh[:, :, h0:h1, :], gain, ALU.mult)

                def b_swapped():
                    for r in range(2):
                        for a, b in ((0, 16), (16, 0)):
                            o, i = 32 * r + a, 32 * r + b
                            v.tensor_tensor(sh[:, :, :, o:o + 16], zbh[:, :, :, i:i + 16],
                                            ROPE[:, 3, :, o:o + 16].unsqueeze(2).broadcast_to([P, NT, QKH, 16]), ALU.mult)

                def b_rotary():
                    v.tensor_tensor(zbh, zbh, ROPE[:, 2].unsqueeze(2).broadcast_to([P, NT, QKH, HD]), ALU.mult)
                    dve.drain()
                    v.tensor_tensor(zbh, zbh, sh, ALU.add).then_inc(b_ready, 1)

                dve.wait_ge(ld_const, 16 * 6)
                dve.wait_ge(ld_attn, (l + 1) * 16 * 8)
                v.tensor_scalar(NSK[:], SK[:], -1.0, None, ALU.mult)
                for i in range(1, ZCH * NT, 2):
                    c, t = i // NT, i % NT
                    copy_out(l, ("z", i), Z[:, t, c * ZC:(c + 1) * ZC], BK[:, bank(("z", i)), 0:ZC])
                    if i > 2 * NT:
                        dve.drain()
                        (b_squares, b_norm, b_swapped, b_rotary)[(i - 2 * NT) // 2]()
                dve.drain()

                def c_squares():
                    freed(dve, l, ("z", ZCH * NT - 2))
                    v.tensor_tensor(SCR_M, zc, zc, ALU.mult)

                def c_sums():
                    v.tensor_reduce(SS[:, LATENTS:LATENTS + 4], SCR_M[:, :, 0:256], AX.X, ALU.add)
                    v.tensor_reduce(SS[:, LATENTS + 4:LATENTS + 8], SCR_M[:, :, 256:384], AX.X, ALU.add)

                def c_norm():
                    for t in range(NT):
                        v.scalar_tensor_tensor(Z[:, t, Z_CQ:Z_CQ + 256], Z[:, t, Z_CQ:Z_CQ + 256],
                                               RST[:, LATENTS + t:LATENTS + t + 1], GC[:, 0:256], ALU.mult, ALU.mult)
                        ins = v.scalar_tensor_tensor(Z[:, t, Z_CKV:Z_CKV + 128], Z[:, t, Z_CKV:Z_CKV + 128],
                                                     RST[:, LATENTS + 4 + t:LATENTS + 5 + t], GC[:, 256:384],
                                                     ALU.mult, ALU.mult)
                    ins.then_inc(c_ready, 1)

                def latents_turned():
                    for k in (0, 2):
                        copy_out(l, ("cT", k), CT[:, k, :], BK[:, bank(("cT", k)), :])

                def latent_queries():
                    for t in range(1, NT, 2):
                        copy_out(l, ("qu", t), QU[:, t, :], BK[:, bank(("qu", t)), 0:NH * MQ])

                def latent_keys():
                    for t in range(1, NT, 2):
                        kv = BK[:, bank(("kv", t)), :].rearrange("p (h n) -> p h n", h=NH)
                        full(dve, l, ("kv", t))
                        v.tensor_copy(KC[:, t, :, 0:HD], kv[:, :, 0:HD])
                        v.tensor_copy(VD[:, t, :].rearrange("p (h n) -> p h n", h=NH), kv[:, :, HD:2 * HD])\
                            .then_inc(dve_free, 1)

                qr = QU.rearrange("p t (h n) -> p t h n", n=MQ)
                kr = Z[:, :, Z_KR:Z_KR + 32]
                sq = SCR_M[:, :, 0:128].rearrange("p t (h n) -> p t h n", n=32)
                sk = SCR_M[:, :, 128:160]

                def d_swapped():
                    freed(dve, l, ("kv", NT - 2))
                    for a, b in ((0, 16), (16, 0)):
                        v.tensor_tensor(sq[:, :, :, a:a + 16], qr[:, :, :, 64 + b:80 + b],
                                        ROPM[:, 1, :, a:a + 16].unsqueeze(2).broadcast_to([P, NT, NH, 16]), ALU.mult)
                        v.tensor_tensor(sk[:, :, a:a + 16], kr[:, :, b:b + 16], ROPM[:, 1, :, a:a + 16], ALU.mult)

                def d_cosines():
                    v.tensor_tensor(qr[:, :, :, 64:96], qr[:, :, :, 64:96],
                                    ROPM[:, 0].unsqueeze(2).broadcast_to([P, NT, NH, 32]), ALU.mult)
                    v.tensor_tensor(kr, kr, ROPM[:, 0], ALU.mult)

                def d_sums():
                    v.tensor_tensor(qr[:, :, :, 64:96], qr[:, :, :, 64:96], sq, ALU.add)
                    for h in range(NH):
                        ins = v.tensor_tensor(KC[:, :, h, HD:MQ], kr, sk, ALU.add)
                    ins.then_inc(qkd_ready, 1)

                between = {0: c_squares, 1: c_sums, 2: lambda: variances([(4, 256), (4, 128)], LATENTS),
                           6: lambda: inverse(l, ROOT_C, 8, LATENTS), 8: c_norm,
                           MLA_AT: latents_turned, MLA_AT + 1: latent_queries, MLA_AT + 2: latent_keys,
                           MLA_AT + 4: d_swapped, MLA_AT + 5: d_cosines, MLA_AT + 6: d_sums}

                def keys(i):
                    if ("kT", i) in INDEX:
                        g, h = HEADS[i]
                        w = MQ if g == 3 else HD
                        dst = KTM[:, h % 2, :] if g == 3 else KT[0:HD, (h // 2) % 2, :]
                        copy_out(l, ("kT", i), dst, BK[0:w, bank(("kT", i)), :])

                def maxima(u):
                    i, t = u // NT, u % NT
                    g, h = HEADS[i]
                    nm = NM[:, i % 2, t:t + 1]
                    if u >= NT:
                        full(dve, l, ("pT", u - NT))
                    dve.wait_ge(s_full, l * UNITS + u + 1)
                    if g in (0, 2):
                        ks = slice(key_tiles(u)[0] * P, (key_tiles(u)[-1] + 1) * P)
                        arrived()
                        v.tensor_tensor_reduce(out=PR[:, t, ks], in0=BK[:, t, ks], in1=MASK[g // 2][:, t, ks],
                                               scale=-HD ** -0.5, scalar=NSK[:, h:h + 1] if g == 0 else -LOWEST,
                                               op0=ALU.add, op1=ALU.min, accum_out=nm).then_inc(s_max, 1)
                    else:
                        v.tensor_reduce(nm, BK[:, t, :], AX.X, ALU.max, negate=True).then_inc(s_max, 1)

                def output(i):
                    g, h = HEADS[i]
                    dve.wait_ge(p_ready, l * UNITS + (i + 1) * NT)
                    if g == 0:
                        v.tensor_tensor(RS[:, i % 2, :], RS[:, i % 2, :], SE[:, i % 2, :], ALU.add)
                        dve.drain()
                    v.reciprocal(RI[:, i % 2, :], RS[:, i % 2, :])
                    dve.drain()
                    dve.wait_ge(o_full, l * UNITS + (i + 1) * NT)
                    half = (h % 2 if g == 3 else h // 2) * HD
                    v.tensor_tensor(Z[:, :, g * GRP + h * HD:g * GRP + (h + 1) * HD], OUT[:, :, half:half + HD],
                                    RI[:, i % 2, :].unsqueeze(2).broadcast_to([P, NT, HD]), ALU.mult).then_inc(o_free, 1)

                def group(step, p):
                    g = HEADS[p * NH][0]
                    if step == "variance":
                        dve.wait_ge(act_sq, l * SUMS_OF_SQUARES + NT + p + 1)
                        variances([(4, GROUP_W)], 4 * p)
                    if step == "norm":
                        inverse(l, ROOT_G + p, 4, 4 * p)
                        for t in range(NT):
                            zo = Z[:, t, g * GRP:g * GRP + GROUP_W]
                            ins = v.scalar_tensor_tensor(zo, zo, RST[:, 4 * p + t:4 * p + t + 1],
                                                         GG[:, g * GROUP_W:(g + 1) * GROUP_W], ALU.mult, ALU.mult)
                        ins.then_inc(y_ready, 1)
                    if step == "turn":
                        k = group_blocks(p)[1]
                        copy_out(l, ("yT", k), HT[:, k, :], BK[:, bank(("yT", k)), :])

                keys(0)
                for u in range(AHEAD):
                    maxima(u)
                for u in range(UNITS):
                    if u % NT == 0 and u // NT + 1 < len(HEADS):
                        keys(u // NT + 1)
                    if u + AHEAD < UNITS:
                        maxima(u + AHEAD)
                    if u in between:
                        dve.drain()
                        between[u]()
                        dve.drain()
                    if group_step(u)[0]:
                        group(*group_step(u))
                    if u % 2 == 0:
                        if u >= 3:
                            dve.wait_ge(o_full, l * UNITS + u - 2)
                        ks = slice(key_tiles(u)[0] * P, (key_tiles(u)[-1] + 1) * P)
                        copy_out(l, ("pT", u), PT[:, u % 3, ks], BK[:, bank(("pT", u)), ks])
                    if u % NT == 0 and u > 0:
                        output(u // NT - 1)
                output(len(HEADS) - 1)

                for step in ("variance", "norm", "turn"):
                    group(step, 3)

                def residual(n):
                    xs = X[:, n // 2, n % 2 * 512:n % 2 * 512 + 512]
                    full(dve, l, ("out", n))
                    v.tensor_tensor(xs, xs, BK[:, bank(("out", n)), :], ALU.add).then_inc(dve_free, 1)

                def second_variance(t):
                    variance(l, NT + 4 + t, t)

                def second_norm(t):
                    normalise(l, ROOT_2 + t, t)

                residual(0)
                residual(1)
                dve.wait_ge(ld_ga, (l + 1) * 32)
                second_variance(0)
                second_norm(0)

                def route_steps(h0=0, h1=PH):
                    lists, heads, hs = range(2 * h0, 2 * h1), range(h0, h1), slice(h0, h1)
                    halves = (slice(0, 8), slice(8, 16))
                    sums = SUMS.rearrange("p h (a b) -> p h a b", a=TOPK)[:, hs]
                    s12 = S12.rearrange("p (h c) k -> p h c k", c=2)[:, hs]
                    i12 = I12F.rearrange("p (h c) k -> p h c k", c=2)[:, hs]
                    full4 = [P, h1 - h0, TOPK, TOPK]
                    full3 = [P, h1 - h0, TOPK]

                    def list_max():
                        for a in lists:
                            v.max(S12[:, a, 0:8], SC[:, a, :])

                    def list_index():
                        for a in lists:
                            v.max_index(I12[:, a, 0:8], S12[:, a, 0:8], SC[:, a, :])

                    def list_rest():
                        for a in lists:
                            ins = v.match_replace(REST[:, a, :], S12[:, a, 0:8], SC[:, a, :], LOWEST)
                        ins.then_inc(sc_used, 1)

                    def rest_max():
                        for a in lists:
                            v.max(S12[:, a, 8:16], REST[:, a, :])

                    def rest_index():
                        for a in lists:
                            v.max_index(I12[:, a, 8:16], S12[:, a, 8:16], REST[:, a, :])

                    def all_sums():
                        v.tensor_tensor(sums, s12[:, :, 0, :].unsqueeze(3).broadcast_to(full4),
                                        s12[:, :, 1, :].unsqueeze(2).broadcast_to(full4), ALU.add)
                        ls = slice(2 * h0, 2 * h1)
                        v.tensor_copy(I12F[:, ls], I12[:, ls])

                    def sum_max(part):
                        for h in heads:
                            v.max(BEST[:, h, halves[part]], SUMS[:, h, :])

                    def sum_index(part):
                        for h in heads:
                            v.max_index(POS[:, h, halves[part]], BEST[:, h, halves[part]], SUMS[:, h, :])

                    def sum_rest():
                        for h in heads:
                            v.match_replace(SUMS[:, h, :], BEST[:, h, 0:8], SUMS[:, h, :], LOWEST)

                    def places():
                        v.tensor_scalar(PAB[:, 0, hs], POS[:, hs], 4, None, ALU.logical_shift_right)
                        v.tensor_scalar(PAB[:, 1, hs], POS[:, hs], 15, None, ALU.bitwise_and)

                    def places_float():
                        v.tensor_copy(PABF[:, :, hs], PAB[:, :, hs])

                    def match(c):
                        v.tensor_tensor(ONE[c][:, hs], IOT[:].unsqueeze(1).unsqueeze(1).broadcast_to(full4),
                                        PABF[:, c, hs].unsqueeze(3).broadcast_to(full4), ALU.is_equal)

                    def pick(c):
                        v.tensor_tensor(ONE[c][:, hs], ONE[c][:, hs], i12[:, :, c, :].unsqueeze(2).broadcast_to(full4),
                                        ALU.mult)

                    def add_up(c):
                        v.tensor_reduce(ISEL[:, c, hs], ONE[c][:, hs], AX.X, ALU.add)

                    def experts():
                        v.scalar_tensor_tensor(EIDX.rearrange("p (h k) -> p h k", h=PH)[:, hs], ISEL[:, 0, hs],
                                               float(PK), ISEL[:, 1, hs], ALU.mult, ALU.add)

                    def rows_and_best():
                        at = slice(h0 * TOPK, h1 * TOPK)
                        if h1 < PH:
                            full(dve, l, ("q0", NQ0 - 2))
                        v.tensor_scalar(IDXU[:, at], EIDX[:, at], LOFF[:, 0:1], None, ALU.add)\
                            .then_inc(idxu_ready, (h0 == 0) + (h1 == PH))
                        ins = v.tensor_tensor(GE[:, hs], BEST[:, hs], BEST[:, hs, 0:1].broadcast_to(full3), ALU.subtract)
                        if h1 == PH:
                            ins.then_inc(best_ready, 1)

                    return [list_max, list_index, list_rest, rest_max, rest_index, all_sums,
                            lambda: sum_max(0), lambda: sum_index(0), sum_rest, lambda: sum_max(1),
                            lambda: sum_index(1), places, places_float, lambda: match(0), lambda: match(1),
                            lambda: pick(0), lambda: pick(1), lambda: add_up(0), lambda: add_up(1), experts,
                            rows_and_best]

                def gates(n):
                    dve.wait_ge(ge_ready, l * (NT + 1) + n + 1)
                    v.tensor_reduce(GSUM, GE, AX.X, ALU.add)
                    dve.drain()
                    v.reciprocal(GSUM, GSUM)
                    dve.drain()
                    v.tensor_tensor(GATE, GE, GSUM.unsqueeze(2).broadcast_to([P, PH, TOPK]), ALU.mult)
                    dve.drain()

                dve.wait_ge(sc_full, l * ROUTES + 1)
                arrived()
                for step in route_steps(0, EARLY):
                    step()
                    dve.drain()

                def other_scores():
                    dve.wait_ge(sc_full, l * ROUTES + 2)
                    arrived()

                def v_rows():
                    v.tensor_scalar(IDXV, EIDX, LOFF[:, 0:1], None, ALU.add).then_inc(idxv_ready, 1)

                aside = {10: [lambda: residual(2)], 14: [lambda: residual(3)], 18: [lambda: residual(4)],
                         20: [lambda: second_variance(1)], 23: [lambda: second_norm(1)], 25: [lambda: residual(5)],
                         29: [lambda: second_variance(2)], 31: [lambda: second_norm(2)], 34: [lambda: residual(6)],
                         40: [lambda: residual(7)], 42: [lambda: second_variance(3)],
                         44: [lambda: second_norm(3)], 64: [lambda: gates(0)]}
                for n, step in enumerate([other_scores] + route_steps(EARLY, PH) + [v_rows]):
                    aside.setdefault(ASIDE_FROM + n, []).extend([dve.drain, step])

                def tile(t, T, rows, aside):
                    dve.drain()
                    dve.wait_ge(h_staged, l * (NT + 1) + t + 1)
                    for s in range(SLOTS):
                        for step in aside.get(s, []):
                            step()
                        dve.wait_ge(slot[s % R], rows + (s // R + 1) * 16)
                        v.tensor_tensor_reduce(out=RING[s % R], in0=RING[s % R], in1=HCUR, scale=1.0, scalar=0.0,
                                               op0=ALU.mult, op1=ALU.add, accum_out=ADOT[:, s:s + 1]).then_inc(used_dve, 1)
                    dve.drain()
                    v.memset(ACC, 0.0).then_inc(u_done, 1)
                    dve.wait_ge(gelu_done, T + 1)
                    v.tensor_tensor(WGT, AGELU, GATE.rearrange("p h k -> p (h k)"), ALU.mult).then_inc(w_ready, 1)
                    steps = route_steps()
                    for s in range(HALF - 1, SLOTS, HALF):
                        dve.drain()
                        dve.wait_ge(slot[s % R], rows + (SLOTS // R + s // R + 1) * 16)
                        v.scalar_tensor_tensor(ACC, RING[s % R], WGT[:, s:s + 1], ACC, ALU.mult, ALU.add)\
                            .then_inc(used_dve, 1)
                        k = s // HALF
                        if k == ROUTE_FROM:
                            dve.wait_ge(sc_full, l * ROUTES + t + 3)
                            arrived()
                        if ROUTE_FROM < k <= ROUTE_FROM + len(steps):
                            steps[k - ROUTE_FROM - 1]()
                    dve.drain()
                    gates(t + 1)
                    dve.wait_ge(used_pe, T * PE_SLOTS + PE_SLOTS + 2 * PE_PER_HALF)
                    v.tensor_scalar(IDXV, EIDX, LOFF[:, 0:1], None, ALU.add).then_inc(idxv_ready, 1)
                    xt = X[:, bass.ds(t, 1), :].rearrange("p a d -> p (a d)")
                    v.tensor_tensor(ACC, ACC, YV, ALU.add).then_inc(v_taken, 1)
                    dve.drain()
                    v.tensor_tensor(xt, xt, ACC, ALU.add)

                tile(0, l * NT, l * (NT * USES * 16), aside)
                with dve.Fori(1, NT) as t:
                    T = dve.snap(l * NT + t)
                    tile(t, T, dve.snap(T * (USES * 16)), {})
                v.tensor_scalar(LOFF[:], LOFF[:], float(NEXP), None, ALU.add)
                dve.drain()
                v.memset(NSK[:], 0.0).then_inc(layer_open, 1)
            dve.wait_ge(ld_gf, 16)
            for t in range(NT):
                variance(DEPTH, t, t)
                normalise(DEPTH, t, t)



def shape_constants():
    import numpy as np
    f = np.float32

    def angles(pos, dim):
        inv = f(10000.0) ** (-np.arange(0, dim, 2, dtype=f) / f(dim))
        ang = pos.astype(f)[:, None] * inv[None, :].astype(f)
        return np.cos(ang).astype(f), np.sin(ang).astype(f)

    pos = np.arange(SEQ)
    c1, s1 = angles(pos, HD)
    cr, sr = angles(pos // 64, HD // 2)
    cc, sc = angles(pos % 64, HD // 2)
    cm, sm = angles(pos, 32)
    cat = lambda *a: np.concatenate(a, axis=1)
    rope = np.stack([cat(c1, c1), cat(-s1, s1), cat(cr, cr, cc, cc), cat(-sr, sr, -sc, sc)]).astype(f)
    rope_m = np.stack([cat(cm, cm), cat(-sm, sm)]).astype(f)
    rel = pos[None, :] - pos[:, None]
    window = np.where(np.abs(rel) <= 128, f(0), f(NEG))
    count = sum(((np.abs(rel) <= w // 2) & (rel % r == 0)).astype(int) for w, r in ((128, 1), (512, 4), (2048, 16)))
    dilated = np.where(count > 0, np.log(np.maximum(count, 1)) * HD ** 0.5, NEG)
    return rope, rope_m, np.stack([window, dilated]).astype(f)


def kernel(**inputs):
    import numpy as _np
    import concourse.bacc as _bacc
    from concourse import mybir as _mybir
    from concourse.bass_utils import run_bass_kernel_spmd as _run

    a = {k: _np.asarray(v) for k, v in inputs.items()}
    rope, rope_m, masks = shape_constants()

    def blocks(w, n):
        k = w.shape[1] // P
        return w.reshape(DEPTH, k, P, n, -1).transpose(0, 3, 2, 1, 4).reshape(DEPTH, n, P, -1)

    feeds = {
        "x": a["x"], "w_in": blocks(a["w_in"], ZCH), "w_out": blocks(a["w_out"], 1)[:, 0],
        "w_q": blocks(a["peer_w_q"], HC), "w_uq": blocks(a["mla_w_uq"], 1)[:, 0], "w_ukv": a["mla_w_ukv"],
        "subk": a["peer_sub_keys"].reshape(DEPTH, HC, PK, P).transpose(0, 3, 1, 2).reshape(DEPTH, P, HC * PK),
        "peer_u": a["peer_u"], "peer_v": a["peer_v"], "g_mix": a["g_mix"], "g_ffn": a["g_ffn"],
        "g_group": a["g_group"].reshape(DEPTH, D), "g_final": a["g_final"].reshape(1, D),
        "g_c": _np.concatenate([a["mla_q_norm"], a["mla_kv_norm"]], axis=1),
        "g_qk": _np.concatenate([a["ax_q_norm"], a["ax_k_norm"]], axis=1),
        "sink": a["win_sink"], "rope": rope, "rope_m": rope_m, "masks": masks,
    }
    nc = _bacc.Bacc("TRN2", target_bir_lowering=False, num_devices=1)
    arrays, args = {}, []
    for name, value in feeds.items():
        value = _np.ascontiguousarray(value)
        arrays[f"in_{name}_dram"] = value
        args.append(nc.dram_tensor(f"in_{name}_dram", value.shape, _mybir.dt.from_np(value.dtype),
                                   kind="ExternalInput").ap())
    out = nc.dram_tensor("out_0_dram", (1, SEQ, D), _mybir.dt.float32, kind="ExternalOutput").ap()
    trunk(nc, *args, out)
    r = _run(nc, [arrays], core_ids=[0])
    return r.results[0]["out_0_dram"]
```
